# Optimizing a Trainium2 kernel written in Bass

```python
import jax, jax.numpy as jnp
from jax import lax
import numpy as np

D_MODEL = 1024
BATCH = 1
SEQ = 256
DEPTH = 2

N_EVEN = (DEPTH + 1) // 2
N_ODD = DEPTH // 2

ROPE_THETA = 10000.0
NORM_EPS = 1e-6

MLA_HEADS = 8
MLA_Q_LORA = 384
MLA_KV_LORA = 256
MLA_NOPE = 64
MLA_ROPE = 32
MLA_V = 64
ATTN_Q_BLOCK = 128

MOBA_HEADS = 8
MOBA_HEAD_DIM = 64
MOBA_BLOCK = 256
MOBA_TOPK = 3
MOBA_Q_CHUNK = 32

MOBA_QKV = 3 * MOBA_HEADS * MOBA_HEAD_DIM
SPLIT_POINTS = (MLA_Q_LORA, MLA_Q_LORA + MLA_KV_LORA, MLA_Q_LORA + MLA_KV_LORA + MLA_ROPE)
D_IN_PROJ = MLA_Q_LORA + MLA_KV_LORA + MLA_ROPE + MOBA_QKV
D_MIX = MLA_HEADS * MLA_V + MOBA_HEADS * MOBA_HEAD_DIM

CONV_WIDTH = 31

PEER_HEADS = 8
PEER_N_KEYS = 128
PEER_N_EXPERTS = PEER_N_KEYS * PEER_N_KEYS
PEER_D_KEY = 256
PEER_D_HALF = PEER_D_KEY // 2
PEER_TOPK = 16
PEER_TOKEN_CHUNK = 128

kernel_name = "hybrid_mla_moba_conformer_peer"

def rms_norm(x, g):
    xf = x.astype(jnp.float32)
    y = xf * lax.rsqrt(jnp.mean(xf * xf, axis=-1, keepdims=True) + NORM_EPS)
    return (y * g.astype(jnp.float32)).astype(x.dtype)

def layer_norm(x, g, b):
    xf = x.astype(jnp.float32)
    mu = jnp.mean(xf, axis=-1, keepdims=True)
    var = jnp.mean(jnp.square(xf - mu), axis=-1, keepdims=True)
    y = (xf - mu) * lax.rsqrt(var + NORM_EPS)
    return (y * g.astype(jnp.float32) + b.astype(jnp.float32)).astype(x.dtype)

def rope_angles(positions, dim):
    inv = 1.0 / (ROPE_THETA ** (jnp.arange(0, dim, 2, dtype=jnp.float32) / dim))
    ang = positions.astype(jnp.float32)[..., None] * inv
    return jnp.cos(ang), jnp.sin(ang)

def apply_rope(x, cos, sin):
    d2 = x.shape[-1] // 2
    x1, x2 = x[..., :d2], x[..., d2:]
    c = cos[:, :, None, :].astype(x.dtype)
    s = sin[:, :, None, :].astype(x.dtype)
    return jnp.concatenate([x1 * c - x2 * s, x2 * c + x1 * s], axis=-1)

def causal_attention_swept(q, k, v, scale):
    B, S, H, dk = q.shape
    nq = S // ATTN_Q_BLOCK
    qb = q.reshape(B, nq, ATTN_Q_BLOCK, H, dk).transpose(1, 0, 2, 3, 4)
    kpos = jnp.arange(S)

    def one_block(args):
        i, qi = args
        s = jnp.einsum('bqhd,bkhd->bhqk', qi, k, preferred_element_type=jnp.float32) * scale
        qpos = i * ATTN_Q_BLOCK + jnp.arange(ATTN_Q_BLOCK)
        s = jnp.where(kpos[None, :] <= qpos[:, None], s, -jnp.inf)
        p = jax.nn.softmax(s, axis=-1).astype(v.dtype)
        return jnp.einsum('bhqk,bkhd->bqhd', p, v)

    o = lax.map(one_block, (jnp.arange(nq), qb))
    return o.transpose(1, 0, 2, 3, 4).reshape(B, S, H, v.shape[-1])

def moba_attention(q, k, v):
    B, S, H, d = q.shape
    nb = -(-S // MOBA_BLOCK)
    pad = nb * MOBA_BLOCK - S
    kp = jnp.pad(k, ((0, 0), (0, pad), (0, 0), (0, 0)))
    vp = jnp.pad(v, ((0, 0), (0, pad), (0, 0), (0, 0)))
    k_blocks = kp.reshape(B, nb, MOBA_BLOCK, H, d).transpose(0, 3, 1, 2, 4)
    v_blocks = vp.reshape(B, nb, MOBA_BLOCK, H, d).transpose(0, 3, 1, 2, 4)
    counts = jnp.minimum(MOBA_BLOCK, S - jnp.arange(nb) * MOBA_BLOCK).astype(jnp.float32)
    k_mean = (k_blocks.astype(jnp.float32).sum(axis=3) / counts[None, None, :, None]).astype(k.dtype)
    topk = min(MOBA_TOPK, nb)
    scale = d ** -0.5
    nc = S // MOBA_Q_CHUNK
    qc = q.reshape(B, nc, MOBA_Q_CHUNK, H, d).transpose(1, 0, 2, 3, 4)
    bidx = jnp.arange(B)[:, None, None, None]
    hidx = jnp.arange(H)[None, :, None, None]
    blk_ids = jnp.arange(nb)

    def one_chunk(args):
        c, qi = args
        qpos = c * MOBA_Q_CHUNK + jnp.arange(MOBA_Q_CHUNK)
        own = (c * MOBA_Q_CHUNK) // MOBA_BLOCK
        gate = jnp.einsum('bqhd,bhnd->bhqn', qi, k_mean, preferred_element_type=jnp.float32)
        gate = jnp.where(blk_ids < own, gate, -jnp.inf)
        _, sel = lax.top_k(gate, topk)
        slot_ok = jnp.arange(topk) < own
        kg = k_blocks[bidx, hidx, sel]
        vg = v_blocks[bidx, hidx, sel]
        s_sel = jnp.einsum('bqhd,bhqjkd->bhqjk', qi, kg, preferred_element_type=jnp.float32) * scale
        s_sel = jnp.where(slot_ok[None, None, None, :, None], s_sel, -jnp.inf)
        ko = lax.dynamic_slice_in_dim(k_blocks, own, 1, axis=2)[:, :, 0]
        vo = lax.dynamic_slice_in_dim(v_blocks, own, 1, axis=2)[:, :, 0]
        s_own = jnp.einsum('bqhd,bhkd->bhqk', qi, ko, preferred_element_type=jnp.float32) * scale
        kpos_own = own * MOBA_BLOCK + jnp.arange(MOBA_BLOCK)
        s_own = jnp.where(kpos_own[None, :] <= qpos[:, None], s_own, -jnp.inf)
        s_all = jnp.concatenate([s_sel.reshape(B, H, MOBA_Q_CHUNK, topk * MOBA_BLOCK), s_own], axis=-1)
        p = jax.nn.softmax(s_all, axis=-1).astype(v.dtype)
        p_sel = p[..., :topk * MOBA_BLOCK].reshape(B, H, MOBA_Q_CHUNK, topk, MOBA_BLOCK)
        p_own = p[..., topk * MOBA_BLOCK:]
        return (jnp.einsum('bhqjk,bhqjkd->bqhd', p_sel, vg)
                + jnp.einsum('bhqk,bhkd->bqhd', p_own, vo))

    o = lax.map(one_chunk, (jnp.arange(nc), qc))
    return o.transpose(1, 0, 2, 3, 4).reshape(B, S, H, d)

def hybrid_attention(hn, w_in, q_norm, w_uq, kv_norm, w_ukv, w_out, cos_r, sin_r, cos_m, sin_m):
    B, S, _ = hn.shape
    proj = hn @ w_in
    c_q, c_kv, k_rope, moba_qkv = jnp.split(proj, SPLIT_POINTS, axis=-1)
    q = (rms_norm(c_q, q_norm) @ w_uq).reshape(B, S, MLA_HEADS, MLA_NOPE + MLA_ROPE)
    q_nope, q_pe = q[..., :MLA_NOPE], q[..., MLA_NOPE:]
    q_pe = apply_rope(q_pe, cos_r, sin_r)
    kv = (rms_norm(c_kv, kv_norm) @ w_ukv).reshape(B, S, MLA_HEADS, MLA_NOPE + MLA_V)
    k_nope, v_mla = kv[..., :MLA_NOPE], kv[..., MLA_NOPE:]
    k_pe = apply_rope(k_rope[:, :, None, :], cos_r, sin_r)
    q_full = jnp.concatenate([q_nope, q_pe], axis=-1)
    k_full = jnp.concatenate([k_nope, jnp.broadcast_to(k_pe, (B, S, MLA_HEADS, MLA_ROPE))], axis=-1)
    o_mla = causal_attention_swept(q_full, k_full, v_mla, (MLA_NOPE + MLA_ROPE) ** -0.5)
    mq, mk, mv = jnp.split(moba_qkv, 3, axis=-1)
    mq = apply_rope(mq.reshape(B, S, MOBA_HEADS, MOBA_HEAD_DIM), cos_m, sin_m)
    mk = apply_rope(mk.reshape(B, S, MOBA_HEADS, MOBA_HEAD_DIM), cos_m, sin_m)
    mv = mv.reshape(B, S, MOBA_HEADS, MOBA_HEAD_DIM)
    o_moba = moba_attention(mq, mk, mv)
    o = jnp.concatenate([o_mla.reshape(B, S, MLA_HEADS * MLA_V),
                         o_moba.reshape(B, S, MOBA_HEADS * MOBA_HEAD_DIM)], axis=-1)
    return o @ w_out

def conformer_conv(hn, w_in, b_in, w_dw, b_dw, ln_g, ln_b, w_out, b_out):
    a = hn @ w_in + b_in
    u, gate = jnp.split(a, 2, axis=-1)
    u = u * jax.nn.sigmoid(gate)
    u = lax.conv_general_dilated(u, w_dw[:, None, :], window_strides=(1,),
                                 padding=((CONV_WIDTH - 1, 0),),
                                 dimension_numbers=('NWC', 'WIO', 'NWC'),
                                 feature_group_count=D_MODEL) + b_dw
    u = jax.nn.silu(layer_norm(u, ln_g, ln_b))
    return u @ w_out + b_out

def peer_ffn(hn, w_q, subkeys, u_tab, v_tab):
    B, S, D = hn.shape
    T = B * S
    xt = hn.reshape(T // PEER_TOKEN_CHUNK, PEER_TOKEN_CHUNK, D)

    def one_chunk(xc):
        q = (xc @ w_q).reshape(PEER_TOKEN_CHUNK, PEER_HEADS, 2, PEER_D_HALF)
        s = jnp.einsum('thcd,hcnd->thcn', q, subkeys, preferred_element_type=jnp.float32)
        s_top, i_top = lax.top_k(s, PEER_TOPK)
        cand = s_top[:, :, 0, :, None] + s_top[:, :, 1, None, :]
        cand_idx = i_top[:, :, 0, :, None] * PEER_N_KEYS + i_top[:, :, 1, None, :]
        best, pos = lax.top_k(cand.reshape(PEER_TOKEN_CHUNK, PEER_HEADS, PEER_TOPK * PEER_TOPK), PEER_TOPK)
        idx = jnp.take_along_axis(cand_idx.reshape(PEER_TOKEN_CHUNK, PEER_HEADS, PEER_TOPK * PEER_TOPK), pos, axis=-1)
        g = jax.nn.softmax(best, axis=-1)
        u = u_tab[idx]
        act = jax.nn.gelu(jnp.einsum('td,thkd->thk', xc, u), approximate=False)
        v = v_tab[idx]
        return jnp.einsum('thk,thkd->td', (g * act).astype(v_tab.dtype), v)

    return lax.map(one_chunk, xt).reshape(B, S, D)

def setup_inputs(seed: int = 0) -> dict:
    key = jax.random.key(seed)
    ks = jax.random.split(key, 24)
    f32 = jnp.float32

    def nrm(k, shape, scale):
        return jax.random.normal(k, shape, f32) * scale

    def gain(k, shape):
        return 1.0 + 0.02 * jax.random.normal(k, shape, f32)

    x = jax.random.normal(ks[0], (BATCH, SEQ, D_MODEL), f32)
    offset = jax.random.randint(ks[1], (BATCH, 1), 0, 4096, dtype=jnp.int32)
    positions = offset + jnp.arange(SEQ, dtype=jnp.int32)[None, :]
    return {
        "x": x,
        "positions": positions,
        "norm_mix": gain(ks[2], (DEPTH, D_MODEL)),
        "norm_ffn": gain(ks[3], (DEPTH, D_MODEL)),
        "norm_final": gain(ks[4], (D_MODEL,)),
        "attn_w_in": nrm(ks[5], (N_EVEN, D_MODEL, D_IN_PROJ), D_MODEL ** -0.5),
        "mla_q_norm": gain(ks[6], (N_EVEN, MLA_Q_LORA)),
        "mla_w_uq": nrm(ks[7], (N_EVEN, MLA_Q_LORA, MLA_HEADS * (MLA_NOPE + MLA_ROPE)), MLA_Q_LORA ** -0.5),
        "mla_kv_norm": gain(ks[8], (N_EVEN, MLA_KV_LORA)),
        "mla_w_ukv": nrm(ks[9], (N_EVEN, MLA_KV_LORA, MLA_HEADS * (MLA_NOPE + MLA_V)), MLA_KV_LORA ** -0.5),
        "attn_w_out": nrm(ks[10], (N_EVEN, D_MIX, D_MODEL), 0.5 * D_MIX ** -0.5),
        "conv_w_in": nrm(ks[11], (N_ODD, D_MODEL, 2 * D_MODEL), D_MODEL ** -0.5),
        "conv_b_in": nrm(ks[12], (N_ODD, 2 * D_MODEL), 0.01),
        "conv_w_dw": nrm(ks[13], (N_ODD, CONV_WIDTH, D_MODEL), CONV_WIDTH ** -0.5),
        "conv_b_dw": nrm(ks[14], (N_ODD, D_MODEL), 0.01),
        "conv_ln_g": gain(ks[15], (N_ODD, D_MODEL)),
        "conv_ln_b": nrm(ks[16], (N_ODD, D_MODEL), 0.01),
        "conv_w_out": nrm(ks[17], (N_ODD, D_MODEL, D_MODEL), 0.5 * D_MODEL ** -0.5),
        "conv_b_out": nrm(ks[18], (N_ODD, D_MODEL), 0.01),
        "peer_w_q": nrm(ks[19], (DEPTH, D_MODEL, PEER_HEADS * PEER_D_KEY), D_MODEL ** -0.5),
        "peer_subkeys": nrm(ks[20], (DEPTH, PEER_HEADS, 2, PEER_N_KEYS, PEER_D_HALF), PEER_D_HALF ** -0.5),
        "peer_u": nrm(ks[21], (DEPTH, PEER_N_EXPERTS, D_MODEL), D_MODEL ** -0.5),
        "peer_v": nrm(ks[22], (DEPTH, PEER_N_EXPERTS, D_MODEL), 0.5 * PEER_HEADS ** -0.5),
    }

def reference(x, positions, norm_mix, norm_ffn, norm_final, attn_w_in, mla_q_norm, mla_w_uq,
              mla_kv_norm, mla_w_ukv, attn_w_out, conv_w_in, conv_b_in, conv_w_dw, conv_b_dw,
              conv_ln_g, conv_ln_b, conv_w_out, conv_b_out, peer_w_q, peer_subkeys, peer_u, peer_v):
    cos_r, sin_r = rope_angles(positions, MLA_ROPE)
    cos_m, sin_m = rope_angles(positions, MOBA_HEAD_DIM)
    h = x
    for layer in range(DEPTH):
        hn = rms_norm(h, norm_mix[layer])
        i = layer // 2
        if layer % 2 == 0:
            mix = hybrid_attention(hn, attn_w_in[i], mla_q_norm[i], mla_w_uq[i], mla_kv_norm[i],
                                   mla_w_ukv[i], attn_w_out[i], cos_r, sin_r, cos_m, sin_m)
        else:
            mix = conformer_conv(hn, conv_w_in[i], conv_b_in[i], conv_w_dw[i], conv_b_dw[i],
                                 conv_ln_g[i], conv_ln_b[i], conv_w_out[i], conv_b_out[i])
        h = h + mix
        h = h + peer_ffn(rms_norm(h, norm_ffn[layer]), peer_w_q[layer], peer_subkeys[layer],
                         peer_u[layer], peer_v[layer])
    return rms_norm(h, norm_final)


_drawn_inputs = setup_inputs


def setup_inputs(seed=0):
    import zlib

    import numpy as np

    out = dict(_drawn_inputs(seed))
    spreads = {}
    factors = {'norm_mix': 4.478,
     'norm_ffn': 12.89,
     'norm_final': 8.263,
     'mla_q_norm': 8.0,
     'mla_kv_norm': 8.0,
     'conv_b_in': 35.354,
     'conv_b_dw': 25.738,
     'conv_ln_g': 27.892,
     'conv_ln_b': 54.053,
     'conv_b_out': 20.115}
    for name, (base, spread) in spreads.items():
        noise = np.random.default_rng([zlib.crc32(name.encode()), seed]).standard_normal(out[name].shape)
        drawn = base * np.exp(spread * noise) if base else spread * noise
        out[name] = __import__('jax').numpy.asarray(drawn.astype(out[name].dtype))
    for name, factor in factors.items():
        out[name] = (out[name] * factor).astype(out[name].dtype)
    return out
```

```python
from contextlib import ExitStack, contextmanager

import numpy as np
import concourse.bass as bass
from concourse import mybir

P = 128
SEQ, D = 256, 1024
TILES = SEQ // P
KD = D // P
LAYERS = 2
EPS = 1e-6
THETA = 10000.0
HEADS = 8
Q_LORA, KV_LORA, NOPE, ROPE, VD = 384, 256, 64, 32, 64
QK = NOPE + ROPE
HD = 64
MOBA = HEADS * HD
OFF_KV, OFF_ROPE = Q_LORA, Q_LORA + KV_LORA
OFF_MQ = OFF_ROPE + ROPE
OFF_MK, OFF_MV = OFF_MQ + MOBA, OFF_MQ + 2 * MOBA
D_IN = OFF_MQ + 3 * MOBA
NQ = HEADS * QK
TAPS = 31
KEYS, TOPK, HALF = 128, 16, 128
EXPERTS = KEYS * KEYS
RING = 8
NF = ROPE // 2 + HD // 2
PHASES = LAYERS * TILES
SLOTS = HEADS * TOPK
CHUNK = 512
PROJ_CHUNKS = [(n, min(CHUNK, D_IN - n)) for n in range(0, D_IN, CHUNK)]
ATTN_HEADS = 2 * HEADS

C_MIX = 0
C_BIN = C_MIX + LAYERS * KD
C_BDW = C_BIN + 2 * KD
C_LNG = C_BDW + KD
C_LNB = C_LNG + KD
C_QN = C_LNB + KD
C_KVN = C_QN + Q_LORA // P
C_TAPS = C_KVN + KV_LORA // P
COLS = C_TAPS + KD * TAPS

K_ID, K_IOTA = 0, P
K_INV = K_IOTA + TOPK
KCOLS = K_INV + NF

N_PROJ, N_NORM = 2 + len(PROJ_CHUNKS), 2
J_C, J_U, J_KV, J_QT, J_KT, J_MQT, J_MKT, J_HEAD = 0, 2, 4, 6, 8, 10, 11, 12
J_OT = J_HEAD + 3 * ATTN_HEADS
J_W = J_OT + 2
N_MIX = J_W + 2
J_GLU, J_ACC, J_Z, J_CW = 2, 2 + KD, 4 + KD, 6 + KD
N_CONV = J_CW + 2
PROJ_AT = [0, N_PROJ]
MIX_AT = [2 * N_PROJ, 2 * N_PROJ + N_MIX + N_NORM]
NORM_AT = [MIX_AT[0] + N_MIX, MIX_AT[1] + N_MIX]
CONV_AT = [NORM_AT[1] + N_NORM, NORM_AT[1] + 2 * N_NORM + N_CONV]
NORM_AT += [CONV_AT[0] + N_CONV, CONV_AT[1] + N_CONV]
BANKS = 3


def build(nc, x_in, pos_in, cols_in, const_in, mask_in, w_in, w_uq, w_ukv, w_out, c_in, c_out, c_bout,
          wq_in, sk_in, gains_in, table, out):
    f32, bf16, i32, u32 = mybir.dt.float32, mybir.dt.bfloat16, mybir.dt.int32, mybir.dt.uint32
    ALU, ACT, AX = mybir.AluOpType, mybir.ActivationFunctionType, mybir.AxisListType
    ctx = ExitStack()
    with ctx:
        def sb(name, words, dt=f32):
            return ctx.enter_context(nc.sbuf_tensor(name, [P, words], dt))

        def sem(name):
            return ctx.enter_context(nc.semaphore(name))

        ident = sb("ident", P)
        ident16 = sb("ident16", P, bf16)
        mask16 = sb("mask16", SEQ, bf16)
        iota16 = sb("iota16", TOPK)
        inv = sb("inv", NF)
        cols = sb("cols", COLS)
        trig = sb("trig", TILES * 2 * NF)
        x = sb("x", TILES * D)
        gain = sb("gain", D)
        hT = sb("hT", D)
        xn = sb("xn", 2 * D)
        junk = sb("junk", D, bf16)
        wq = sb("wq", KD * 2 * HALF)
        skT = sb("skT", 2 * KEYS)
        ring = sb("ring", RING * 2 * D)

        def xt(t):
            return x[:, t * D:(t + 1) * D]

        xn_ = xn[:, 0:D]
        xnT = xn[:, D:2 * D].rearrange("p (k t) -> p k t", k=KD)
        hT_ = hT[:, :].rearrange("p (k t) -> p k t", k=KD)
        wq_ = wq[:, :].rearrange("p (k n) -> p k n", k=KD)
        win_ = [ring[:, n * KD:(n + w) * KD].rearrange("p (k n) -> p k n", k=KD) if w == CHUNK
                else xn[:, 0:w * KD].rearrange("p (k n) -> p k n", k=KD) for n, w in PROJ_CHUNKS]

        size = dict(uq=3 * NQ, ukv=2 * D, wout=KD * D, proj=TILES * D_IN, vmla=TILES * MOBA, qT=HEADS * P,
                    mqT=HEADS // 2 * P, kT=HEADS * SEQ, mkT=HEADS // 2 * SEQ, pp=4 * SEQ, o=D, sums=2 * ATTN_HEADS)
        conv_size = dict(cin=KD * 2 * D, cout=KD * CHUNK, cb=CHUNK, uT=KD * (TAPS - 1 + SEQ), acc=D, v=D)
        arena = sb("arena", max(sum(size.values()), sum(conv_size.values())))
        at, part = 0, {}
        for k, n in size.items():
            part[k] = arena[:, at:at + n]
            at += n
        at = 0
        for k, n in conv_size.items():
            part[k] = arena[:, at:at + n]
            at += n
        uq = part["uq"].rearrange("p (k n) -> p k n", n=NQ)
        ukv = part["ukv"].rearrange("p (k n) -> p k n", n=D)
        wout = part["wout"].rearrange("p (k n) -> p k n", n=D)
        proj = [part["proj"][:, t * D_IN:(t + 1) * D_IN] for t in range(TILES)]
        vmla = [part["vmla"][:, t * MOBA:(t + 1) * MOBA] for t in range(TILES)]
        qT = part["qT"].rearrange("p (h t) -> p h t", h=HEADS)
        mqT = part["mqT"].rearrange("p (h t) -> p h t", h=HEADS // 2)
        kT = part["kT"].rearrange("p (h t) -> p h t", h=HEADS)
        mkT = part["mkT"].rearrange("p (h t) -> p h t", h=HEADS // 2)
        kfull = part["pp"][:, 0:NQ].rearrange("p (h d) -> p h d", h=HEADS)
        rtmp = [part[k][:, NQ:NQ + 256] for k in ("pp", "o")]
        pb = [part["pp"][:, i * SEQ:(i + 1) * SEQ] for i in range(2)]
        pT = [part["pp"][:, (2 + i) * SEQ:(3 + i) * SEQ].rearrange("p (k t) -> p k t", k=TILES) for i in range(2)]
        o = part["o"]
        qsb = o[:, 0:NQ]
        cT = hT_
        cin = part["cin"].rearrange("p (j k n) -> p j k n", j=4, k=KD)
        cout = part["cout"].rearrange("p (k n) -> p k n", k=KD)
        cbias = part["cb"]
        uT = part["uT"].rearrange("p (c t) -> p c t", c=KD)
        acc = part["acc"].rearrange("p (c t) -> p c t", c=KD)
        v = part["v"]
        sig = [part["acc"][:, i * P:(i + 1) * P] for i in range(2)]

        qq = sb("qq", 4 * P)
        q_t, q_T, eq = qq[:, 0:2 * P], qq[:, 2 * P:4 * P], qq
        sc = sb("sc", 2 * KEYS)
        sc2 = sb("sc2", 2 * KEYS)
        top = sb("top", 2 * TOPK)
        topi = sb("topi", 2 * TOPK, u32)
        topf = sb("topf", 2 * TOPK)
        best = sb("best", TOPK)
        pos = sb("pos", TOPK, u32)
        pos2 = sb("pos2", 2 * TOPK, u32)
        sel = sb("sel", 2 * TOPK)
        idx = [sb(f"idx{i}", RING, u32) for i in range(TOPK // RING)]
        nbest = sb("nbest", 1)
        e_g = sb("e_g", TOPK)
        e_sum = sb("e_sum", 1)
        e_inv = sb("e_inv", 1)
        g_next = sb("g_next", TOPK)
        g_cur = sb("g_cur", TOPK)
        dot = sb("dot", TOPK)
        gel = sb("gel", TOPK)
        coef = sb("coef", TOPK)
        diag = sb("diag", 2 * P)
        small = sb("small", 16)
        smalli = sb("smalli", 2, i32)
        posi = sb("posi", TILES, i32)
        posf = sb("posf", TILES)
        rows, rinv = part["sums"][:, 0:ATTN_HEADS], part["sums"][:, ATTN_HEADS:2 * ATTN_HEADS]
        nmax = small[:, 14:16]

        ypsum = ctx.enter_context(nc.psum_tensor("ypsum", [P, D], f32))
        qpsum = ctx.enter_context(nc.psum_tensor("qpsum", [P, CHUNK], f32))
        tpsum = ctx.enter_context(nc.psum_tensor("tpsum", [P, CHUNK], f32))
        spsum = ctx.enter_context(nc.psum_tensor("spsum", [P, CHUNK], f32))
        banks = [ctx.enter_context(nc.psum_tensor(f"bank{b}", [P, CHUNK], f32)) for b in range(BANKS)]

        consts_in = sem("consts_in")
        x_loaded = [sem(f"x_loaded{t}") for t in range(TILES)]
        win_in = [sem(f"win_in{n}") for n in range(len(PROJ_CHUNKS))]
        uq_in, ukv_in, wout_in = sem("uq_in"), sem("ukv_in"), sem("wout_in")
        wq_loaded, gain_in = sem("wq_loaded"), sem("gain_in")
        cin_in = [sem(f"cin_in{j}") for j in range(4)]
        cout_in = sem("cout_in")
        out_sent = sem("out_sent")
        bank_full = [sem(f"bank_full{b}") for b in range(BANKS)]
        bank_free = [sem(f"bank_free{b}") for b in range(BANKS)]
        dve_step, act_step = sem("dve_step"), sem("act_step")
        hn_ready, xn_ready = sem("hn_ready"), sem("xn_ready")
        cn_ready, rope_ready, qpe_ready = sem("cn_ready"), sem("rope_ready"), sem("qpe_ready")
        max_ready, o_ready, x_mixed = sem("max_ready"), sem("o_ready"), sem("x_mixed")
        sig_ready, acc_ready, z_ready, half_done = sem("sig_ready"), sem("acc_ready"), sem("z_ready"), sem("half_done")
        q_ready, q_copied, qT_ready, qT_copied = sem("q_ready"), sem("q_copied"), sem("qT_ready"), sem("qT_copied")
        s_ready, s_copied = sem("s_ready"), sem("s_copied")
        routed = [sem(f"routed{i}") for i in range(TOPK // RING)]
        best_ready, exp_ready, g_ready, g_taken = sem("best_ready"), sem("exp_ready"), sem("g_ready"), sem("g_taken")
        dot_ready, diag_ready, v_used = sem("dot_ready"), sem("diag_ready"), sem("v_used")
        ring_free, settled = sem("ring_free"), sem("settled")
        row_in = [sem(f"row_in{b}") for b in range(RING)]
        y_taken, final_ready, id_ready = sem("y_taken"), sem("final_ready"), sem("id_ready")

        def full(eng, j):
            eng.wait_ge(bank_full[j % BANKS], j // BANKS + 1)

        def emptied(eng, j):
            eng.wait_ge(bank_free[j % BANKS], j // BANKS + 1)

        def bank_of(eng, j):
            if j >= BANKS:
                eng.wait_ge(bank_free[j % BANKS], j // BANKS)
            return banks[j % BANKS]

        def held(eng, signal, count):
            if not (isinstance(count, int) and count == 0):
                eng.wait_ge(signal, count)

        def settle(eng):
            eng.sem_inc(settled, 1)

        class Own:

            def __init__(self, eng, signal):
                self.eng, self.sem, self.n, self.turn = eng, signal, 0, 0

            def did(self, ins):
                ins.then_inc(self.sem, 1)
                self.n += 1

            def wait(self, back=0):
                self.eng.wait_ge(self.sem, self.turn + (self.n - back))

            def then(self, ins):
                self.did(ins)
                self.wait()

            @contextmanager
            def loop(self, i, times, per):
                start = self.n
                self.turn = i * per
                yield
                assert self.n - start == per, self.n - start
                self.turn, self.n = 0, start + per * times

        block = ctx.enter_context(nc.Block())

        @block.sync
        def _(sp):
            sp.dma_start(xt(0), x_in[0:P, :]).then_inc(x_loaded[0], 16)
            for dst, src in ((ident[:, :], const_in[:, K_ID:K_ID + P]), (iota16[:, :], const_in[:, K_IOTA:K_IOTA + TOPK]),
                             (inv[:, :], const_in[:, K_INV:K_INV + NF]), (cols[:, :], cols_in[:, :]),
                             (eq[:, 0:SEQ], mask_in[:, :]), (posi[:, :], pos_in[:, :])):
                sp.dma_start(dst, src).then_inc(consts_in, 16)
            w_in_ = w_in.rearrange("(k p) n -> p k n", p=P)
            for c, (n, w) in enumerate(PROJ_CHUNKS):
                sp.dma_start(win_[c], w_in_[:, :, n:n + w]).then_inc(win_in[c], 16)
                if c == 0:
                    sp.dma_start(xt(1), x_in[P:SEQ, :]).then_inc(x_loaded[1], 16)
            sp.dma_start(uq, w_uq.rearrange("(k p) n -> p k n", p=P)).then_inc(uq_in, 16)
            sp.dma_start(ukv, w_ukv.rearrange("(k p) n -> p k n", p=P)).then_inc(ukv_in, 16)
            sp.dma_start(wout, w_out.rearrange("(k p) n -> p k n", p=P)).then_inc(wout_in, 16)

            def load_gain(n):
                sp.dma_start(gain[:, :], gains_in[n:n + 1, :].to_broadcast([P, D])).then_inc(gain_in, 16)

            def load_head(layer, h):
                sp.dma_start(wq_, wq_in[layer].rearrange("(k p) n -> p k n", p=P)[:, :, bass.ds(h * 2 * HALF, 2 * HALF)])\
                  .then_inc(wq_loaded, 16)
                sp.dma_start(skT[:, :], sk_in[layer][:, bass.ds(h * 2 * KEYS, 2 * KEYS)]).then_inc(wq_loaded, 16)

            def load_conv_out(n):
                if n:
                    sp.wait_ge(half_done, n)
                cs = (n % 2) * CHUNK
                sp.dma_start(cout, c_out.rearrange("(k p) n -> p k n", p=P)[:, :, cs:cs + CHUNK]).then_inc(cout_in, 16)
                sp.dma_start(cbias, c_bout[0:1, cs:cs + CHUNK].to_broadcast([P, CHUNK])).then_inc(cout_in, 16)

            load_gain(0)
            for p in range(PHASES):
                layer = p // TILES
                if p == 0:
                    load_head(0, 0)
                else:
                    sp.wait_ge(s_ready, p * HEADS)
                    load_head(layer, 0)
                if p == TILES:
                    sp.wait_ge(xn_ready, TILES)
                    load_gain(1)
                with sp.Fori(1, HEADS) as h:
                    sp.wait_ge(s_ready, h + p * HEADS)
                    load_head(layer, h)
                if p == 0:
                    sp.wait_ge(x_mixed, TILES)
                    cw = c_in.rearrange("(k p) n -> p k n", p=P)
                    for j in range(4):
                        for g in range(2):
                            sp.dma_start(cin[:, j, :, g * 256:(g + 1) * 256], cw[:, :, g * D + j * 256:g * D + (j + 1) * 256])\
                              .then_inc(cin_in[j], 16)
                    load_conv_out(0)
                if p in (1, 2):
                    for n in (2 * p - 1, 2 * p):
                        if n < 4:
                            load_conv_out(n)
            sp.wait_ge(xn_ready, PHASES)
            load_gain(2)
            for t in range(TILES):
                sp.wait_ge(final_ready, t + 1)
                sp.dma_start(out[t * P:(t + 1) * P, :], xt(t)).then_inc(out_sent, 16)
            sp.wait_ge(out_sent, 16 * TILES)

        @block.gpsimd
        def _(pool):
            pool.sem_inc(ring_free, RING)
            for p in range(PHASES):
                with pool.Fori(0, HEADS) as h:
                    for k in range(TOPK):
                        if k % RING == 0:
                            pool.wait_ge(routed[k // RING], h + (p * HEADS + 1))
                        b = k % RING
                        pool.wait_ge(ring_free, h * TOPK + (p * SLOTS + k + 1))
                        settle(pool)
                        pool.indirect_dma_start(
                            out=ring[:, b * 2 * D:(b + 1) * 2 * D], out_offset=None, in_=table[:, :],
                            in_offset=bass.IndirectOffsetOnAxis(ap=idx[k // RING][:, b:b + 1], axis=0)).then_inc(row_in[b], 16)

        @block.tensor
        def _(pe):
            def mm(o_, l, r, start, stop, **kw):
                return nc.tensor.matmul(o_, l, r, start=start, stop=stop, **kw)

            def transposes(j, srcs, rows_=P):
                bank = bank_of(pe, j)
                for i, s in enumerate(srcs):
                    last = nc.tensor.transpose(bank[0:rows_, i * P:(i + 1) * P], s, ident[:, :])
                last.then_inc(bank_full[j % BANKS], 1)

            def turn_over(j, src):
                for i in range(2):
                    transposes(j + i, [src[:, (4 * i + k) * P:(4 * i + k + 1) * P] for k in range(4)])

            def gemm(j, lhs, rhs, width):
                bank = bank_of(pe, j)
                for k, (l, r) in enumerate(zip(lhs, rhs)):
                    last = mm(bank[:, 0:width], l, r, k == 0, k == len(lhs) - 1)
                last.then_inc(bank_full[j % BANKS], 1)

            def project(t):
                J = PROJ_AT[t]
                pe.wait_ge(hn_ready, t + 1)
                turn_over(J, o)
                emptied(pe, J)
                emptied(pe, J + 1)
                for c, (n, w) in enumerate(PROJ_CHUNKS):
                    if t == 0:
                        pe.wait_ge(win_in[c], 16)
                    gemm(J + 2 + c, [hT_[:, k, :] for k in range(KD)], [win_[c][:, k, :] for k in range(KD)], w)

            def mix_products(t):
                J = MIX_AT[t]
                pe.wait_ge(cn_ready, t + 1)
                transposes(J + J_C, [proj[t][:, i * P:(i + 1) * P] for i in range(3)])
                transposes(J + J_C + 1, [proj[t][:, OFF_KV + i * P:OFF_KV + (i + 1) * P] for i in range(2)])
                emptied(pe, J + J_C)
                pe.wait_ge(uq_in, 16)
                for i, w in enumerate((CHUNK, NQ - CHUNK)):
                    gemm(J + J_U + i, [cT[:, k, :] for k in range(3)],
                         [uq[:, k, i * CHUNK:i * CHUNK + w] for k in range(3)], w)
                emptied(pe, J + J_C + 1)
                pe.wait_ge(ukv_in, 16)
                for i in range(2):
                    gemm(J + J_KV + i, [cT[:, 3 + k, :] for k in range(2)],
                         [ukv[:, k, i * CHUNK:(i + 1) * CHUNK] for k in range(2)], CHUNK)
                pe.wait_ge(qpe_ready, t + 1)
                for i in range(2):
                    transposes(J + J_QT + i, [qsb[:, (4 * i + h) * QK:(4 * i + h + 1) * QK] for h in range(4)], QK)
                emptied(pe, J + J_KV)
                for i in range(2):
                    transposes(J + J_KT + i, [kfull[:, 4 * i + h, :] for h in range(4)], QK)
                pe.wait_ge(rope_ready, t + 1)
                transposes(J + J_MQT, [proj[t][:, OFF_MQ + i * P:OFF_MQ + (i + 1) * P] for i in range(4)])
                transposes(J + J_MKT, [proj[t][:, OFF_MK + i * P:OFF_MK + (i + 1) * P] for i in range(4)])

            def mix_heads(t):
                J = MIX_AT[t] + J_HEAD
                W = (t + 1) * P

                def scores(a):
                    j = J + 3 * a
                    bank = bank_of(pe, j)
                    mm(bank[:, 0:W], ident16[:, :], mask16[:, SEQ - W:SEQ], True, False)
                    if a < HEADS:
                        l, r = qT[0:QK, a, :], kT[0:QK, a, 0:W]
                    else:
                        b, s = (a - HEADS) // 2, HD * (a % 2)
                        l, r = mqT[s:s + HD, b, :], mkT[s:s + HD, b, 0:W]
                    mm(bank[:, 0:W], l, r, False, True).then_inc(bank_full[j % BANKS], 1)

                def values(a, s):
                    return vmla[s][:, a * VD:(a + 1) * VD] if a < HEADS else \
                        proj[s][:, OFF_MV + (a - HEADS) * HD:OFF_MV + (a - HEADS + 1) * HD]

                for i in range(MIX_AT[t] + J_QT, MIX_AT[t] + J_HEAD):
                    emptied(pe, i)
                scores(0)
                for a in range(ATTN_HEADS):
                    emptied(pe, J + 3 * a)
                    transposes(J + 3 * a + 1, [pb[a % 2][:, s * P:(s + 1) * P] for s in range(t + 1)])
                    if a + 1 < ATTN_HEADS:
                        scores(a + 1)
                    emptied(pe, J + 3 * a + 1)
                    gemm(J + 3 * a + 2, [pT[a % 2][:, s, :] for s in range(t + 1)], [values(a, s) for s in range(t + 1)], VD)

            def mix_out(t):
                J = MIX_AT[t]
                pe.wait_ge(o_ready, t + 1)
                turn_over(J + J_OT, o)
                emptied(pe, J + J_OT)
                emptied(pe, J + J_OT + 1)
                pe.wait_ge(wout_in, 16)
                for i in range(2):
                    gemm(J + J_W + i, [hT_[:, k, :] for k in range(KD)],
                         [wout[:, k, i * CHUNK:(i + 1) * CHUNK] for k in range(KD)], CHUNK)

            def conv_glu(t):
                J = CONV_AT[t]
                pe.wait_ge(hn_ready, TILES + t + 1)
                turn_over(J, v)
                emptied(pe, J)
                emptied(pe, J + 1)
                for c in range(KD):
                    if t == 0 and c % 2 == 0:
                        pe.wait_ge(cin_in[c // 2], 32)
                    j = J + J_GLU + c
                    bank = bank_of(pe, j)
                    for g in range(2):
                        cs = g * 256 + (c % 2) * P
                        for k in range(KD):
                            last = mm(bank[:, g * P:(g + 1) * P], cin[:, c // 2, k, cs:cs + P], hT_[:, k, :], k == 0, k == KD - 1)
                    last.then_inc(bank_full[j % BANKS], 1)

            def conv_out(t):
                J = CONV_AT[t]
                pe.wait_ge(acc_ready, t + 1)
                turn_over(J + J_ACC, part["acc"])
                pe.wait_ge(z_ready, t + 1)
                turn_over(J + J_Z, v)
                emptied(pe, J + J_Z)
                emptied(pe, J + J_Z + 1)
                for i in range(2):
                    pe.wait_ge(cout_in, 32 * (2 * t + i + 1))
                    gemm(J + J_CW + i, [hT_[:, k, :] for k in range(KD)], [cout[:, k, :] for k in range(KD)], CHUNK)

            def peer_q(H):
                pe.wait_ge(wq_loaded, (H + 1) * 32)
                held(pe, q_copied, H)
                for k in range(KD):
                    last = mm(qpsum[:, 0:2 * HALF], xnT[:, k, :], wq_[:, k, :], k == 0, k == KD - 1)
                last.then_inc(q_ready, 1)

            def peer_qT(H):
                pe.wait_ge(q_copied, H + 1)
                held(pe, qT_copied, H)
                for c in range(2):
                    last = nc.tensor.transpose(tpsum[:, c * P:(c + 1) * P], q_t[:, c * HALF:(c + 1) * HALF], ident[:, :])
                last.then_inc(qT_ready, 1)

            def peer_scores(H):
                pe.wait_ge(qT_copied, H + 1)
                held(pe, s_copied, H)
                for c in range(2):
                    last = mm(spsum[:, c * KEYS:(c + 1) * KEYS], q_T[:, c * P:(c + 1) * P], skT[:, c * KEYS:(c + 1) * KEYS], True, True)
                last.then_inc(s_ready, 1)

            def peer_slot(H, k, stop=False):
                pe.wait_ge(diag_ready, H * TOPK + (k + 1))
                b = k % RING
                for half in range(2):
                    last = mm(ypsum[:, half * CHUNK:(half + 1) * CHUNK], diag[:, (k % 2) * P:(k % 2 + 1) * P],
                              ring[:, b * 2 * D + D + half * CHUNK:b * 2 * D + D + (half + 1) * CHUNK], False, stop,
                              skip_group_check=True)
                last.then_inc(ring_free, 1)

            def peer_start(p):
                pe.wait_ge(xn_ready, p + 1)
                turn_over(NORM_AT[p], xn_)
                emptied(pe, NORM_AT[p])
                emptied(pe, NORM_AT[p] + 1)
                if p:
                    pe.wait_ge(y_taken, p)
                for half in range(2):
                    mm(ypsum[:, half * CHUNK:(half + 1) * CHUNK], ident[:, :],
                       xt(p % TILES)[:, half * CHUNK:(half + 1) * CHUNK], True, False, skip_group_check=True)
                peer_q(p * HEADS)
                peer_qT(p * HEADS)
                peer_scores(p * HEADS)

            def peer(p):
                with pe.Fori(0, HEADS - 1) as h:
                    for k in range(TOPK):
                        peer_slot(h + p * HEADS, k)
                        if k == 1:
                            peer_q(h + (p * HEADS + 1))
                        if k == 3:
                            peer_qT(h + (p * HEADS + 1))
                        if k == 5:
                            peer_scores(h + (p * HEADS + 1))
                for k in range(TOPK):
                    peer_slot((p + 1) * HEADS - 1, k, stop=k == TOPK - 1)

            pe.wait_ge(consts_in, 6 * 16)
            pe.wait_ge(id_ready, 1)
            project(0)
            project(1)
            for t in range(TILES):
                mix_products(t)
                mix_heads(t)
                mix_out(t)
                peer_start(t)
                peer(t)
            for t in range(TILES):
                conv_glu(t)
                conv_out(t)
                peer_start(TILES + t)
                peer(TILES + t)

        @block.scalar
        def _(act):
            own = Own(act, act_step)

            def run(out_, in_, func=ACT.Copy, **kw):
                return nc.scalar.activation(out_, in_, func, **kw)

            def free(j, ins):
                ins.then_inc(bank_free[j % BANKS], 1)

            def take(j, out_, n=CHUNK, rows_=P, **kw):
                full(act, j)
                free(j, run(out_, banks[j % BANKS][0:rows_, 0:n], **kw))

            def take_scaled(j, dst, k0, count, col):
                full(act, j)
                for i in range(count):
                    last = run(dst[:, k0 + i, :], banks[j % BANKS][:, i * P:(i + 1) * P], scale=cols[:, col + i:col + i + 1])
                free(j, last)

            def project(t):
                J = PROJ_AT[t]
                for i in range(2):
                    take_scaled(J + i, hT_, 4 * i, 4, C_MIX + 4 * i)
                for c, (n, w) in enumerate(PROJ_CHUNKS):
                    take(J + 2 + c, proj[t][:, n:n + w], w)

            def mix_products(t):
                J = MIX_AT[t]
                if t:
                    act.wait_ge(x_mixed, t)
                take_scaled(J + J_C, cT, 0, 3, C_QN)
                take_scaled(J + J_C + 1, cT, 3, 2, C_KVN)
                take(J + J_U, qsb[:, 0:CHUNK])
                take(J + J_U + 1, qsb[:, CHUNK:NQ], NQ - CHUNK)
                full(act, J + J_KV)
                free(J + J_KV, run(kfull[:, :, 0:NOPE], banks[(J + J_KV) % BANKS][:, :].rearrange("p (h d) -> p h d", h=HEADS)))
                take(J + J_KV + 1, vmla[t])
                for i in range(2):
                    take(J + J_QT + i, qT[0:QK, 4 * i:4 * i + 4, :].rearrange("p h t -> p (h t)"), rows_=QK, scale=QK ** -0.5)

                def keys(j, dst, rows_):
                    full(act, j)
                    free(j, run(dst, banks[j % BANKS][0:rows_, :].rearrange("p (h t) -> p h t", h=4)))
                for i in range(2):
                    keys(J + J_KT + i, kT[0:QK, 4 * i:4 * i + 4, t * P:(t + 1) * P], QK)
                take(J + J_MQT, mqT[:, :, :].rearrange("p h t -> p (h t)"), scale=HD ** -0.5)
                keys(J + J_MKT, mkT[:, :, t * P:(t + 1) * P], P)

            def mix_heads(t):
                J = MIX_AT[t] + J_HEAD
                W = (t + 1) * P
                for a in range(ATTN_HEADS):
                    act.wait_ge(max_ready, t * ATTN_HEADS + a + 1)
                    if a >= 2:
                        emptied(act, J + 3 * (a - 2) + 1)
                    free(J + 3 * a, run(pb[a % 2][:, 0:W], banks[(J + 3 * a) % BANKS][:, 0:W], ACT.Exp,
                                        bias=nmax[:, a % 2:a % 2 + 1], accum_out=rows[:, a:a + 1]))

            def mix_out(t):
                J = MIX_AT[t] + J_OT
                for i in range(2):
                    take(J + i, hT[:, i * CHUNK:(i + 1) * CHUNK])

            def conv_glu(t):
                J = CONV_AT[t]
                if t:
                    act.wait_ge(half_done, 2 * t)
                for i in range(2):
                    take_scaled(J + i, hT_, 4 * i, 4, C_MIX + KD + 4 * i)
                for c in range(KD):
                    j = J + J_GLU + c
                    full(act, j)
                    if c >= 2:
                        emptied(act, j - 2)
                    run(sig[c % 2], banks[j % BANKS][:, P:2 * P], ACT.Sigmoid,
                        bias=cols[:, C_BIN + KD + c:C_BIN + KD + c + 1]).then_inc(sig_ready, 1)

            def conv_out(t):
                J = CONV_AT[t]
                for i in range(2):
                    take(J + J_ACC + i, v[:, i * CHUNK:(i + 1) * CHUNK])
                for i in range(2):
                    j = J + J_Z + i
                    full(act, j)
                    for k in range(4):
                        c = 4 * i + k
                        last = run(hT_[:, c, :], banks[j % BANKS][:, k * P:(k + 1) * P], ACT.Silu,
                                   scale=cols[:, C_LNG + c:C_LNG + c + 1], bias=cols[:, C_LNB + c:C_LNB + c + 1])
                    free(j, last)

            def peer_copy(H, ready, copied, dst, psum, used):
                act.wait_ge(ready, H + 1)
                held(act, used, H)
                if dst is q_t:
                    held(act, routed[0], H)
                run(dst[:, :], psum[:, 0:2 * P]).then_inc(copied, 1)

            def peer_exp(H):
                act.wait_ge(best_ready, H + 1)
                run(e_g[:, :], best[:, :], ACT.Exp, bias=nbest[:, 0:1], accum_out=e_sum[:, 0:1]).then_inc(exp_ready, 1)

            def peer_gates(H):
                act.wait_ge(g_ready, H + 1)
                run(g_cur[:, :], g_next[:, :]).then_inc(g_taken, 1)
                act.wait_ge(g_taken, H + 1)

            def peer_slot(H, k, first=False):
                act.wait_ge(dot_ready, H * TOPK + (k + 1))
                own.then(run(gel[:, k:k + 1], dot[:, k:k + 1], ACT.Gelu))
                own.then(run(coef[:, k:k + 1], gel[:, k:k + 1], scale=g_cur[:, k:k + 1]))
                if not (first and k < 2):
                    act.wait_ge(ring_free, H * TOPK + (k - 1 + RING))
                run(diag[:, (k % 2) * P:(k % 2 + 1) * P], ident[:, :], scale=coef[:, k:k + 1]).then_inc(diag_ready, 1)

            def peer_start(p):
                for i in range(2):
                    take(NORM_AT[p] + i, xn[:, D + i * CHUNK:D + (i + 1) * CHUNK])
                H = p * HEADS
                peer_copy(H, q_ready, q_copied, q_t, qpsum, qT_ready)
                peer_copy(H, qT_ready, qT_copied, q_T, tpsum, s_ready)
                peer_copy(H, s_ready, s_copied, sc, spsum, routed[0])
                peer_exp(H)

            def peer(p):
                with act.Fori(0, HEADS - 1) as h:
                    H, N = h + p * HEADS, h + (p * HEADS + 1)
                    with own.loop(h, HEADS - 1, 2 * TOPK):
                        peer_gates(H)
                        for k in range(TOPK):
                            peer_slot(H, k)
                            if k == 1:
                                peer_copy(N, q_ready, q_copied, q_t, qpsum, qT_ready)
                            if k == 3:
                                peer_copy(N, qT_ready, qT_copied, q_T, tpsum, s_ready)
                            if k == 5:
                                peer_copy(N, s_ready, s_copied, sc, spsum, routed[0])
                            if k == 9:
                                peer_exp(N)
                H = (p + 1) * HEADS - 1
                peer_gates(H)
                for k in range(TOPK):
                    peer_slot(H, k)

            act.wait_ge(consts_in, 6 * 16)
            act.wait_ge(id_ready, 2)
            run(trig[:, :], trig[:, :], ACT.Sin).then_inc(id_ready, 1)
            project(0)
            project(1)
            for t in range(TILES):
                mix_products(t)
                mix_heads(t)
                mix_out(t)
                peer_start(t)
                peer(t)
            for t in range(TILES):
                conv_glu(t)
                conv_out(t)
                peer_start(TILES + t)
                peer(TILES + t)

        @block.vector
        def _(dve):
            own = Own(dve, dve_step)
            V = nc.vector

            def free(j, ins):
                ins.then_inc(bank_free[j % BANKS], 1)

            def power(var, w, y, tmp):
                yi, vi = y.bitcast(i32), var.bitcast(i32)
                own.then(V.tensor_scalar(smalli[:, 0:w], vi, 1, None, ALU.logical_shift_right))
                own.then(V.tensor_scalar(yi, smalli[:, 0:w], -1.0, float(0x5f3759df), ALU.mult, ALU.add))
                for _ in range(4):
                    own.then(V.tensor_tensor(tmp, y, y, ALU.mult))
                    own.then(V.tensor_tensor(tmp, tmp, var, ALU.mult))
                    own.then(V.tensor_scalar(tmp, tmp, -0.5, 1.5, ALU.mult, ALU.add))
                    own.then(V.tensor_tensor(y, y, tmp, ALU.mult))

            def mean_square(src, n, c):
                own.then(V.tensor_tensor_reduce(out=junk[:, 0:n], in0=src, in1=src, scale=1.0, scalar=0.0,
                                                op0=ALU.mult, op1=ALU.add, accum_out=small[:, c:c + 1]))
                own.then(V.tensor_scalar(small[:, c:c + 1], small[:, c:c + 1], 1.0 / n, EPS, ALU.mult, ALU.add))

            def rms(src, n):
                mean_square(src, n, 0)
                power(small[:, 0:1], 1, small[:, 2:3], small[:, 4:5])
                return small[:, 2:3]

            def project(t):
                dve.wait_ge(x_loaded[t], 16)
                r = rms(xt(t), D)
                if t:
                    emptied(dve, PROJ_AT[t - 1] + 1)
                V.tensor_scalar(o, xt(t), r, None, ALU.mult).then_inc(hn_ready, 1)

            def rotate(src, heads, half, t, f0):
                c = trig[:, t * 2 * NF + f0:t * 2 * NF + f0 + half].unsqueeze(1).to_broadcast([P, heads, half])
                s = trig[:, t * 2 * NF + NF + f0:t * 2 * NF + NF + f0 + half].unsqueeze(1).to_broadcast([P, heads, half])
                x1, x2 = src[:, :, 0:half], src[:, :, half:2 * half]
                a, b = (r[:, 0:heads * half].rearrange("p (h d) -> p h d", h=heads) for r in rtmp)
                own.did(V.tensor_tensor(a, x1, s, ALU.mult))
                own.then(V.tensor_tensor(b, x2, s, ALU.mult))
                own.did(V.tensor_tensor(x1, x1, c, ALU.mult))
                own.then(V.tensor_tensor(x2, x2, c, ALU.mult))
                own.did(V.tensor_tensor(x1, x1, b, ALU.subtract))
                own.then(V.tensor_tensor(x2, x2, a, ALU.add))

            def mix_products(t):
                J = MIX_AT[t]
                for c in range(len(PROJ_CHUNKS)):
                    emptied(dve, PROJ_AT[t] + 2 + c)
                mean_square(proj[t][:, 0:Q_LORA], Q_LORA, 0)
                mean_square(proj[t][:, OFF_KV:OFF_ROPE], KV_LORA, 1)
                power(small[:, 0:2], 2, small[:, 2:4], small[:, 4:6])
                V.tensor_scalar(proj[t][:, 0:Q_LORA], proj[t][:, 0:Q_LORA], small[:, 2:3], None, ALU.mult)
                V.tensor_scalar(proj[t][:, OFF_KV:OFF_ROPE], proj[t][:, OFF_KV:OFF_ROPE], small[:, 3:4], None, ALU.mult)\
                 .then_inc(cn_ready, 1)
                dve.wait_ge(id_ready, 3)
                if t == 0:
                    emptied(dve, PROJ_AT[1] + 1)
                rotate(proj[t][:, OFF_ROPE:OFF_MQ].unsqueeze(1), 1, ROPE // 2, t, 0)
                own.did(V.tensor_copy(kfull[:, :, NOPE:QK], proj[t][:, OFF_ROPE:OFF_MQ].unsqueeze(1).to_broadcast([P, HEADS, ROPE])))
                for off in (OFF_MQ, OFF_MK):
                    rotate(proj[t][:, off:off + MOBA].rearrange("p (h d) -> p h d", h=HEADS), HEADS, HD // 2, t, ROPE // 2)
                dve.sem_inc(rope_ready, 1)
                for i in range(2):
                    emptied(dve, J + J_U + i)
                rotate(qsb.rearrange("p (h d) -> p h d", h=HEADS)[:, :, NOPE:QK], HEADS, ROPE // 2, t, 0)
                dve.sem_inc(qpe_ready, 1)

            def mix_heads(t):
                J = MIX_AT[t] + J_HEAD
                W = (t + 1) * P

                def maximum(a):
                    j = J + 3 * a
                    full(dve, j)
                    V.tensor_reduce(nmax[:, a % 2:a % 2 + 1], banks[j % BANKS][:, 0:W], AX.X, ALU.max, negate=True)\
                     .then_inc(max_ready, 1)

                maximum(0)
                for a in range(ATTN_HEADS):
                    j = J + 3 * a + 1
                    full(dve, j)
                    if a == 0:
                        emptied(dve, MIX_AT[t] + J_KT + 1)
                    free(j, V.tensor_copy(pT[a % 2][:, 0:t + 1, :].rearrange("p s t -> p (s t)"), banks[j % BANKS][:, 0:W]))
                    if a + 1 < ATTN_HEADS:
                        maximum(a + 1)
                    own.then(V.reciprocal(rinv[:, a:a + 1], rows[:, a:a + 1]))
                    full(dve, j + 1)
                    ins = V.tensor_scalar(o[:, a * VD:(a + 1) * VD], banks[(j + 1) % BANKS][:, 0:VD], rinv[:, a:a + 1], None, ALU.mult)
                    free(j + 1, ins)
                emptied(dve, J + 3 * (ATTN_HEADS - 1) + 2)
                dve.sem_inc(o_ready, 1)

            def mix_out(t):
                for i in range(2):
                    j = MIX_AT[t] + J_W + i
                    full(dve, j)
                    xs = xt(t)[:, i * CHUNK:(i + 1) * CHUNK]
                    free(j, V.tensor_tensor(xs, xs, banks[j % BANKS][:, :], ALU.add))
                for i in range(2):
                    emptied(dve, MIX_AT[t] + J_W + i)
                dve.sem_inc(x_mixed, 1)

            def conv_glu(t):
                J = CONV_AT[t]
                r = rms(xt(t), D)
                if t:
                    dve.wait_ge(half_done, 2 * t)
                V.tensor_scalar(v, xt(t), r, None, ALU.mult).then_inc(hn_ready, 1)
                if t == 0:
                    own.did(V.memset(uT[:, :, 0:TAPS - 1], 0.0))
                for c in range(KD):
                    j = J + J_GLU + c
                    dve.wait_ge(sig_ready, t * KD + c + 1)
                    full(dve, j)
                    free(j, V.scalar_tensor_tensor(out=uT[:, c, TAPS - 1 + t * P:TAPS - 1 + (t + 1) * P],
                                                   in0=banks[j % BANKS][:, 0:P], scalar=cols[:, C_BIN + c:C_BIN + c + 1],
                                                   in1=sig[c % 2], op0=ALU.add, op1=ALU.mult))

            def conv_taps(t):
                for c in range(KD):
                    emptied(dve, CONV_AT[t] + J_GLU + c)
                for c in range(KD):
                    own.did(V.tensor_scalar(acc[:, c, :], uT[:, c, t * P:(t + 1) * P], cols[:, C_TAPS + c * TAPS:C_TAPS + c * TAPS + 1],
                                            cols[:, C_BDW + c:C_BDW + c + 1], ALU.mult, ALU.add))
                with dve.Fori(1, TAPS) as k:
                    with own.loop(k - 1, TAPS - 1, KD):
                        for c in range(KD):
                            own.wait(KD - 1)
                            own.did(V.scalar_tensor_tensor(
                                out=acc[:, c, :], in0=uT[:, c, bass.ds(k + t * P, P)],
                                scalar=cols[:, bass.ds(k + (C_TAPS + c * TAPS), 1)], in1=acc[:, c, :], op0=ALU.mult, op1=ALU.add))
                own.wait()
                dve.sem_inc(acc_ready, 1)

            def conv_norm(t):
                J = CONV_AT[t]
                for i in range(2):
                    emptied(dve, J + J_ACC + i)
                    own.did(V.bn_stats(small[:, 0:6] if i == 0 else eqs, v[:, i * CHUNK:(i + 1) * CHUNK]))
                own.wait()
                own.then(V.bn_aggr(small[:, 12:14], small[:, 0:12]))
                own.then(V.tensor_scalar(small[:, 0:1], small[:, 13:14], EPS, None, ALU.add))
                power(small[:, 0:1], 1, small[:, 2:3], small[:, 4:5])
                V.tensor_scalar(v, v, small[:, 12:13], small[:, 2:3], ALU.subtract, ALU.mult).then_inc(z_ready, 1)

            eqs = small[:, 6:12]

            def conv_out(t):
                for i in range(2):
                    j = CONV_AT[t] + J_CW + i
                    full(dve, j)
                    xs = xt(t)[:, i * CHUNK:(i + 1) * CHUNK]
                    free(j, V.tensor_tensor(xs, xs, banks[j % BANKS][:, :], ALU.add))
                    emptied(dve, j)
                    V.tensor_tensor(xs, xs, cbias, ALU.add).then_inc(half_done, 1)
                    dve.wait_ge(half_done, 2 * t + i + 1)

            def route(H, layer, part_):
                top_, topi_, topf_ = (r[:, :].rearrange("p (c k) -> p c k", c=2) for r in (top, topi, topf))
                sc_, sc2_ = (r[:, :].rearrange("p (c k) -> p c k", c=2) for r in (sc, sc2))
                low = -3.0e38
                if part_ == 0:
                    dve.wait_ge(s_copied, H + 1)
                    settle(dve)
                    for c in range(2):
                        own.did(V.max(top_[:, c, 0:8], sc_[:, c, :]))
                    for c in range(2):
                        own.wait(1)
                        settle(dve)
                        own.did(V.max_index(topi_[:, c, 0:8], top_[:, c, 0:8], sc_[:, c, :]))
                        own.did(V.match_replace(sc2_[:, c, :], top_[:, c, 0:8], sc_[:, c, :], low))
                    own.wait()
                if part_ == 1:
                    settle(dve)
                    for c in range(2):
                        own.did(V.max(top_[:, c, 8:16], sc2_[:, c, :]))
                    for c in range(2):
                        own.wait(1)
                        settle(dve)
                        own.did(V.max_index(topi_[:, c, 8:16], top_[:, c, 8:16], sc2_[:, c, :]))
                    own.wait()
                    own.did(V.tensor_scalar(topf_[:, 0, :], topi_[:, 0, :], float(layer * KEYS), None, ALU.add))
                    own.did(V.tensor_copy(topf_[:, 1, :], topi_[:, 1, :]))
                cand, cand2 = sc2, sc
                if part_ == 2:
                    own.then(V.tensor_tensor(cand[:, :].rearrange("p (a b) -> p a b", a=TOPK),
                                             top_[:, 0, :].unsqueeze(2).to_broadcast([P, TOPK, TOPK]),
                                             top_[:, 1, :].unsqueeze(1).to_broadcast([P, TOPK, TOPK]), ALU.add))
                    settle(dve)
                    own.then(V.max(best[:, 0:8], cand[:, :]))
                    settle(dve)
                    own.did(V.max_index(pos[:, 0:8], best[:, 0:8], cand[:, :]))
                    own.then(V.match_replace(cand2[:, :], best[:, 0:8], cand[:, :], low))
                if part_ == 3:
                    settle(dve)
                    own.then(V.max(best[:, 8:16], cand2[:, :]))
                    settle(dve)
                    own.did(V.max_index(pos[:, 8:16], best[:, 8:16], cand2[:, :]))
                    V.tensor_scalar(nbest[:, :], best[:, 0:1], -1.0, None, ALU.mult).then_inc(best_ready, 1)
                    own.wait()
                    own.did(V.tensor_scalar(pos2[:, 0:TOPK], pos[:, :], 4, None, ALU.logical_shift_right))
                    own.then(V.tensor_scalar(pos2[:, TOPK:2 * TOPK], pos[:, :], TOPK - 1, None, ALU.bitwise_and))
                eq_ = eq[:, :].rearrange("p (c k a) -> p (c k) a", c=2, k=TOPK)
                eq4 = eq[:, :].rearrange("p (c k a) -> p c k a", c=2, k=TOPK)
                if part_ == 4:
                    own.then(V.tensor_tensor(eq_, pos2[:, :].unsqueeze(2).to_broadcast([P, 2 * TOPK, TOPK]),
                                             iota16[:, :].unsqueeze(1).to_broadcast([P, 2 * TOPK, TOPK]), ALU.is_equal))
                    own.then(V.tensor_tensor(eq4, eq4, topf_.unsqueeze(2).to_broadcast([P, 2, TOPK, TOPK]), ALU.mult))
                    own.then(V.tensor_reduce(sel[:, :], eq_, AX.X, ALU.add))
                if part_ in (5, 7):
                    i = (part_ - 5) // 2
                    V.scalar_tensor_tensor(out=idx[i][:, :], in0=sel[:, i * RING:(i + 1) * RING], scalar=float(KEYS),
                                           in1=sel[:, TOPK + i * RING:TOPK + (i + 1) * RING],
                                           op0=ALU.mult, op1=ALU.add).then_inc(routed[i], 1)
                if part_ == 6:
                    dve.wait_ge(exp_ready, H + 1)
                    own.then(V.reciprocal(e_inv[:, :], e_sum[:, :]))
                    held(dve, g_taken, H)
                    V.tensor_scalar(g_next[:, :], e_g[:, :], e_inv[:, :], None, ALU.mult).then_inc(g_ready, 1)

            OWN_PER_ROUTE = 6 + 6 + 4 + 4 + 3 + 1

            def dots(H, k):
                b = k % RING
                dve.wait_ge(row_in[b], H * 32 + 16 * (k // RING + 1))
                V.tensor_tensor_reduce(out=junk[:, :], in0=xn_, in1=ring[:, b * 2 * D:b * 2 * D + D], scale=1.0, scalar=0.0,
                                       op0=ALU.mult, op1=ALU.add, accum_out=dot[:, k:k + 1]).then_inc(dot_ready, 1)
                dve.wait_ge(dot_ready, H * TOPK + (k + 1))

            def peer_start(p):
                r = rms(xt(p % TILES), D)
                dve.wait_ge(gain_in, 16 * (p // TILES + 1))
                if p:
                    dve.wait_ge(s_ready, p * HEADS)
                V.scalar_tensor_tensor(out=xn_, in0=xt(p % TILES), scalar=r, in1=gain[:, :], op0=ALU.mult, op1=ALU.mult)\
                 .then_inc(xn_ready, 1)
                dve.wait_ge(xn_ready, p + 1)
                for part_ in range(8):
                    route(p * HEADS, p // TILES, part_)

            def peer(p):
                layer = p // TILES
                with dve.Fori(0, HEADS - 1) as h:
                    with own.loop(h, HEADS - 1, OWN_PER_ROUTE):
                        for k in range(TOPK):
                            dots(h + p * HEADS, k)
                            if 6 <= k < 13:
                                route(h + (p * HEADS + 1), layer, k - 6)
                        route(h + (p * HEADS + 1), layer, 7)
                for k in range(TOPK):
                    dots((p + 1) * HEADS - 1, k)

            def peer_end(p):
                dve.wait_ge(ring_free, RING + (p + 1) * SLOTS)
                V.tensor_copy(xt(p % TILES), ypsum[:, :]).then_inc(y_taken, 1)
                dve.wait_ge(y_taken, p + 1)

            def final(t):
                r = rms(xt(t), D)
                dve.wait_ge(gain_in, 16 * 3)
                V.scalar_tensor_tensor(out=xt(t), in0=xt(t), scalar=r, in1=gain[:, :], op0=ALU.mult, op1=ALU.mult)\
                 .then_inc(final_ready, 1)

            dve.wait_ge(consts_in, 6 * 16)
            own.did(V.tensor_copy(mask16[:, :], eq[:, 0:SEQ]))
            V.tensor_copy(ident16[:, :], ident[:, :]).then_inc(id_ready, 1)
            own.then(V.tensor_copy(posf[:, :], posi[:, :]))
            C1 = 6.28125
            C2 = float(np.float32(np.int32(np.float64(2 * np.pi - C1) * 2 ** 20) / 2 ** 20))
            C3 = float(np.float32(2 * np.pi - C1 - C2))
            magic = 12582912.0
            turns, ang = eq[:, 256:256 + 2 * NF], eq[:, 384:384 + 2 * NF]
            for t in range(TILES):
                for c in range(2):
                    own.did(V.tensor_scalar(ang[:, c * NF:(c + 1) * NF], inv[:, :], posf[:, t:t + 1], None, ALU.mult))
                own.wait()
                for c, quarter in ((0, 0.25), (1, 0.0)):
                    s = slice(c * NF, (c + 1) * NF)
                    own.then(V.tensor_scalar(turns[:, s], ang[:, s], float(1 / (2 * np.pi)), quarter, ALU.mult, ALU.add))
                    own.then(V.tensor_scalar(turns[:, s], turns[:, s], magic, -magic, ALU.add, ALU.add))
                    for part_ in (C1, C2, C3):
                        own.then(V.scalar_tensor_tensor(out=ang[:, s], in0=turns[:, s], scalar=-part_, in1=ang[:, s], op0=ALU.mult, op1=ALU.add))
                    if c == 0:
                        own.then(V.tensor_scalar(ang[:, s], ang[:, s], float(np.pi / 2), None, ALU.add))
                own.then(V.tensor_scalar(trig[:, t * 2 * NF:(t + 1) * 2 * NF], ang, 3.1415925, -3.1415925, ALU.min, ALU.max))
            dve.sem_inc(id_ready, 1)
            project(0)
            project(1)
            for t in range(TILES):
                mix_products(t)
                mix_heads(t)
                mix_out(t)
                peer_start(t)
                peer(t)
                peer_end(t)
            for t in range(TILES):
                conv_glu(t)
                conv_taps(t)
                conv_norm(t)
                conv_out(t)
                peer_start(TILES + t)
                peer(TILES + t)
                peer_end(TILES + t)
            for t in range(TILES):
                final(t)


def kernel(**inputs):
    import concourse.bacc as bacc
    from concourse.bass_utils import run_bass_kernel_spmd

    a = {k: np.asarray(v) for k, v in inputs.items()}

    def split(w):
        return np.ascontiguousarray(w.reshape(-1, P).T)

    taps = a["conv_w_dw"][0].reshape(TAPS, KD, P).transpose(2, 1, 0).reshape(P, KD * TAPS)
    cols = np.concatenate([split(a["norm_mix"]), split(a["conv_b_in"]), split(a["conv_b_dw"]), split(a["conv_ln_g"]),
                           split(a["conv_ln_b"]), split(a["mla_q_norm"]), split(a["mla_kv_norm"]), taps], axis=1)
    f = np.float32
    inv = np.concatenate([f(1.0) / (f(THETA) ** (np.arange(0, d, 2, dtype=f) / f(d))) for d in (ROPE, HD)])
    const = np.concatenate([np.eye(P, dtype=f), np.tile(np.arange(TOPK, dtype=f), (P, 1)), np.tile(inv.astype(f), (P, 1))], axis=1)
    mask = np.concatenate([np.zeros((P, P), f), np.triu(np.full((P, P), -1e30, f), 1)], axis=1)
    ukv = a["mla_w_ukv"][0].reshape(KV_LORA, HEADS, 2, NOPE).transpose(0, 2, 1, 3).reshape(KV_LORA, D)
    arrays = {
        "x": a["x"].reshape(SEQ, D),
        "positions": np.ascontiguousarray(a["positions"].reshape(TILES, P).T),
        "cols": cols, "const": const, "mask": mask,
        "w_in": a["attn_w_in"][0], "w_uq": a["mla_w_uq"][0], "w_ukv": ukv, "w_out": a["attn_w_out"][0],
        "c_in": a["conv_w_in"][0], "c_out": a["conv_w_out"][0], "c_bout": a["conv_b_out"],
        "wq": a["peer_w_q"],
        "sk": a["peer_subkeys"].transpose(0, 4, 1, 2, 3).reshape(LAYERS, HALF, HEADS * 2 * KEYS),
        "gains": np.concatenate([a["norm_ffn"], a["norm_final"].reshape(1, D)], axis=0),
        "table": np.concatenate([a["peer_u"], a["peer_v"]], axis=2).reshape(LAYERS * EXPERTS, 2 * D),
    }
    arrays = {k: np.ascontiguousarray(v) for k, v in arrays.items()}
    nc = bacc.Bacc("TRN2", target_bir_lowering=False, num_devices=1)
    args = [nc.dram_tensor(f"{k}_dram", v.shape, mybir.dt.from_np(v.dtype), kind="ExternalInput").ap() for k, v in arrays.items()]
    out = nc.dram_tensor("out_dram", (SEQ, D), mybir.dt.float32, kind="ExternalOutput").ap()
    build(nc, *args, out)
    r = run_bass_kernel_spmd(nc, [{f"{k}_dram": v for k, v in arrays.items()}], core_ids=[0])
    return r.results[0]["out_dram"].reshape(1, SEQ, D)
```

```python
from contextlib import ExitStack, contextmanager

import numpy as np
import concourse.bass as bass
from concourse import mybir

P = 128
SEQ, D = 256, 1024
TILES = SEQ // P
KD = D // P
LAYERS = 2
EPS = 1e-6
THETA = 10000.0
HEADS = 8
Q_LORA, KV_LORA, NOPE, ROPE, VD = 384, 256, 64, 32, 64
QK = NOPE + ROPE
HD = 64
MOBA = HEADS * HD
OFF_KV, OFF_ROPE = Q_LORA, Q_LORA + KV_LORA
OFF_MQ = OFF_ROPE + ROPE
OFF_MK, OFF_MV = OFF_MQ + MOBA, OFF_MQ + 2 * MOBA
D_IN = OFF_MQ + 3 * MOBA
NQ = HEADS * QK
TAPS = 31
KEYS, TOPK, HALF = 128, 16, 128
EXPERTS = KEYS * KEYS
RING = 8
NF = ROPE // 2 + HD // 2
PHASES = LAYERS * TILES
SLOTS = HEADS * TOPK
CHUNK = 512
PROJ_CHUNKS = [(n, min(CHUNK, D_IN - n)) for n in range(0, D_IN, CHUNK)]
ATTN_HEADS = 2 * HEADS

C_MIX = 0
C_BIN = C_MIX + LAYERS * KD
C_BDW = C_BIN + 2 * KD
C_LNG = C_BDW + KD
C_LNB = C_LNG + KD
C_QN = C_LNB + KD
C_KVN = C_QN + Q_LORA // P
C_TAPS = C_KVN + KV_LORA // P
COLS = C_TAPS + KD * TAPS

K_ID, K_IOTA = 0, P
K_INV = K_IOTA + TOPK
KCOLS = K_INV + NF

N_PROJ, N_NORM = 2 + len(PROJ_CHUNKS), 2
J_C, J_U, J_KV, J_QT, J_KT, J_MQT, J_MKT, J_HEAD = 0, 2, 4, 6, 8, 10, 11, 12
J_OT = J_HEAD + 3 * ATTN_HEADS
J_W = J_OT + 2
N_MIX = J_W + 2
J_GLU, J_ACC, J_Z, J_CW = 2, 2 + KD, 4 + KD, 6 + KD
N_CONV = J_CW + 2
PROJ_AT = [0, N_PROJ]
MIX_AT = [2 * N_PROJ, 2 * N_PROJ + N_MIX + N_NORM]
NORM_AT = [MIX_AT[0] + N_MIX, MIX_AT[1] + N_MIX]
CONV_AT = [NORM_AT[1] + N_NORM, NORM_AT[1] + 2 * N_NORM + N_CONV]
NORM_AT += [CONV_AT[0] + N_CONV, CONV_AT[1] + N_CONV]
BANKS = 3


def build(nc, x_in, pos_in, cols_in, const_in, mask_in, w_in, w_uq, w_ukv, w_out, c_in, c_out, c_bout,
          wq_in, sk_in, gains_in, table, out):
    f32, bf16, i32, u32 = mybir.dt.float32, mybir.dt.bfloat16, mybir.dt.int32, mybir.dt.uint32
    ALU, ACT, AX = mybir.AluOpType, mybir.ActivationFunctionType, mybir.AxisListType
    ctx = ExitStack()
    with ctx:
        def sb(name, words, dt=f32):
            return ctx.enter_context(nc.sbuf_tensor(name, [P, words], dt))

        def sem(name):
            return ctx.enter_context(nc.semaphore(name))

        ident = sb("ident", P)
        ident16 = sb("ident16", P, bf16)
        mask16 = sb("mask16", SEQ, bf16)
        iota16 = sb("iota16", TOPK)
        inv = sb("inv", NF)
        cols = sb("cols", COLS)
        trig = sb("trig", TILES * 2 * NF)
        x = sb("x", TILES * D)
        hT = sb("hT", D)
        xns = sb("xns", 3 * D)
        junk = sb("junk", D, bf16)
        wq = sb("wq", KD * 2 * HALF)
        skT = sb("skT", 2 * KEYS)
        ring = sb("ring", RING * 2 * D)

        def xt(t):
            return x[:, t * D:(t + 1) * D]

        xn = [xns[:, 0:D], xns[:, 2 * D:3 * D]]
        xnT_ = xns[:, D:2 * D]
        xnT = xnT_.rearrange("p (k t) -> p k t", k=KD)
        hT_ = hT[:, :].rearrange("p (k t) -> p k t", k=KD)
        wq_ = wq[:, :].rearrange("p (k n) -> p k n", k=KD)
        win_ = [ring[:, n * KD:(n + w) * KD].rearrange("p (k n) -> p k n", k=KD) if w == CHUNK
                else xns[:, D:D + w * KD].rearrange("p (k n) -> p k n", k=KD) for n, w in PROJ_CHUNKS]

        size = dict(uq=3 * NQ, ukv=2 * D, wout=KD * D, proj=TILES * D_IN, vmla=TILES * MOBA, qT=HEADS * P,
                    mqT=HEADS // 2 * P, kT=HEADS * SEQ, mkT=HEADS // 2 * SEQ, pp=4 * SEQ, o=D, sums=2 * ATTN_HEADS)
        conv_size = dict(cin=KD * 2 * D, cout=KD * CHUNK, cb=CHUNK, uT=KD * (TAPS - 1 + SEQ), acc=D, v=D)
        arena = sb("arena", max(sum(size.values()), sum(conv_size.values())))
        at, part = 0, {}
        for k, n in size.items():
            part[k] = arena[:, at:at + n]
            at += n
        at = 0
        for k, n in conv_size.items():
            part[k] = arena[:, at:at + n]
            at += n
        uq = part["uq"].rearrange("p (k n) -> p k n", n=NQ)
        ukv = part["ukv"].rearrange("p (k n) -> p k n", n=D)
        wout = part["wout"].rearrange("p (k n) -> p k n", n=D)
        proj = [part["proj"][:, t * D_IN:(t + 1) * D_IN] for t in range(TILES)]
        vmla = [part["vmla"][:, t * MOBA:(t + 1) * MOBA] for t in range(TILES)]
        qT = part["qT"].rearrange("p (h t) -> p h t", h=HEADS)
        mqT = part["mqT"].rearrange("p (h t) -> p h t", h=HEADS // 2)
        kT = part["kT"].rearrange("p (h t) -> p h t", h=HEADS)
        mkT = part["mkT"].rearrange("p (h t) -> p h t", h=HEADS // 2)
        kfull = part["pp"][:, 0:NQ].rearrange("p (h d) -> p h d", h=HEADS)
        rtmp = [part[k][:, NQ:NQ + 256] for k in ("pp", "o")]
        pb = [part["pp"][:, i * SEQ:(i + 1) * SEQ] for i in range(2)]
        pT = [part["pp"][:, (2 + i) * SEQ:(3 + i) * SEQ].rearrange("p (k t) -> p k t", k=TILES) for i in range(2)]
        o = part["o"]
        qsb = o[:, 0:NQ]
        cT = hT_
        cin = part["cin"].rearrange("p (j k n) -> p j k n", j=4, k=KD)
        cout = part["cout"].rearrange("p (k n) -> p k n", k=KD)
        cbias = part["cb"]
        uT = part["uT"].rearrange("p (c t) -> p c t", c=KD)
        acc = part["acc"].rearrange("p (c t) -> p c t", c=KD)
        v = part["v"]
        sig = [part["acc"][:, i * P:(i + 1) * P] for i in range(2)]

        qq = sb("qq", 4 * P)
        q_t, q_T, eq = qq[:, 0:2 * P], qq[:, 2 * P:4 * P], qq
        sc = sb("sc", 2 * KEYS)
        sc2 = sb("sc2", 2 * KEYS)
        top = sb("top", 2 * TOPK)
        topi = sb("topi", 2 * TOPK, u32)
        topf = sb("topf", 2 * TOPK)
        best = sb("best", TOPK)
        pos = sb("pos", TOPK, u32)
        pos2 = sb("pos2", 2 * TOPK, u32)
        sel = sb("sel", 2 * TOPK)
        idx = [sb(f"idx{i}", RING, u32) for i in range(TOPK // RING)]
        nbest = sb("nbest", 1)
        e_g = sb("e_g", TOPK)
        e_sum = sb("e_sum", 1)
        e_inv = sb("e_inv", 1)
        g_next = sb("g_next", TOPK)
        g_cur = sb("g_cur", TOPK)
        dot = sb("dot", TOPK)
        gel = sb("gel", TOPK)
        coef = sb("coef", TOPK)
        diag = sb("diag", 2 * P)
        small = sb("small", 16)
        smalli = sb("smalli", 2, i32)
        posi = sb("posi", TILES, i32)
        posf = sb("posf", TILES)
        rows, rinv = part["sums"][:, 0:ATTN_HEADS], part["sums"][:, ATTN_HEADS:2 * ATTN_HEADS]
        nmax = small[:, 14:16]

        ypsum = ctx.enter_context(nc.psum_tensor("ypsum", [P, D], f32))
        qpsum = ctx.enter_context(nc.psum_tensor("qpsum", [P, CHUNK], f32))
        tpsum = ctx.enter_context(nc.psum_tensor("tpsum", [P, CHUNK], f32))
        spsum = ctx.enter_context(nc.psum_tensor("spsum", [P, CHUNK], f32))
        banks = [ctx.enter_context(nc.psum_tensor(f"bank{b}", [P, CHUNK], f32)) for b in range(BANKS)]

        consts_in = sem("consts_in")
        x_loaded = [sem(f"x_loaded{t}") for t in range(TILES)]
        win_in = [sem(f"win_in{n}") for n in range(len(PROJ_CHUNKS))]
        uq_in, ukv_in, wout_in = sem("uq_in"), sem("ukv_in"), sem("wout_in")
        wq_loaded = sem("wq_loaded")
        gain_in = [sem(f"gain_in{i}") for i in range(2)]
        cin_in = [sem(f"cin_in{j}") for j in range(4)]
        cout_in = sem("cout_in")
        out_sent = sem("out_sent")
        bank_full = [sem(f"bank_full{b}") for b in range(BANKS)]
        bank_free = [sem(f"bank_free{b}") for b in range(BANKS)]
        dve_step, act_step = sem("dve_step"), sem("act_step")
        hn_ready, xn_ready = sem("hn_ready"), sem("xn_ready")
        cn_ready, rope_ready, qpe_ready = sem("cn_ready"), sem("rope_ready"), sem("qpe_ready")
        max_ready, o_ready, x_mixed = sem("max_ready"), sem("o_ready"), sem("x_mixed")
        sig_ready, acc_ready, z_ready, half_done = sem("sig_ready"), sem("acc_ready"), sem("z_ready"), sem("half_done")
        q_ready, q_copied, qT_ready, qT_copied = sem("q_ready"), sem("q_copied"), sem("qT_ready"), sem("qT_copied")
        s_ready, s_copied = sem("s_ready"), sem("s_copied")
        routed = [sem(f"routed{i}") for i in range(TOPK // RING)]
        best_ready, exp_ready, g_ready, g_taken = sem("best_ready"), sem("exp_ready"), sem("g_ready"), sem("g_taken")
        dot_ready, diag_ready, v_used = sem("dot_ready"), sem("diag_ready"), sem("v_used")
        ring_free, settled = sem("ring_free"), sem("settled")
        row_in = [sem(f"row_in{b}") for b in range(RING)]
        y_taken, final_ready, id_ready = sem("y_taken"), sem("final_ready"), sem("id_ready")

        def full(eng, j):
            eng.wait_ge(bank_full[j % BANKS], j // BANKS + 1)

        def emptied(eng, j):
            eng.wait_ge(bank_free[j % BANKS], j // BANKS + 1)

        def bank_of(eng, j):
            if j >= BANKS:
                eng.wait_ge(bank_free[j % BANKS], j // BANKS)
            return banks[j % BANKS]

        def held(eng, signal, count):
            if not (isinstance(count, int) and count == 0):
                eng.wait_ge(signal, count)

        def settle(eng):
            eng.sem_inc(settled, 1)

        class Own:

            def __init__(self, eng, signal):
                self.eng, self.sem, self.n, self.turn = eng, signal, 0, 0

            def did(self, ins):
                ins.then_inc(self.sem, 1)
                self.n += 1

            def wait(self, back=0):
                self.eng.wait_ge(self.sem, self.turn + (self.n - back))

            def then(self, ins):
                self.did(ins)
                self.wait()

            @contextmanager
            def loop(self, i, times, per):
                start = self.n
                self.turn = i * per
                yield
                assert self.n - start == per, self.n - start
                self.turn, self.n = 0, start + per * times

        def load_conv_out(eng, n):
            if n:
                eng.wait_ge(half_done, n)
            cs = (n % 2) * CHUNK
            eng.dma_start(cout, c_out.rearrange("(k p) n -> p k n", p=P)[:, :, cs:cs + CHUNK]).then_inc(cout_in, 16)
            eng.dma_start(cbias, c_bout[0:1, cs:cs + CHUNK].to_broadcast([P, CHUNK])).then_inc(cout_in, 16)

        block = ctx.enter_context(nc.Block())

        @block.sync
        def _(sp):
            sp.dma_start(xt(0), x_in[0:P, :]).then_inc(x_loaded[0], 16)
            for dst, src in ((ident[:, :], const_in[:, K_ID:K_ID + P]), (iota16[:, :], const_in[:, K_IOTA:K_IOTA + TOPK]),
                             (inv[:, :], const_in[:, K_INV:K_INV + NF]), (cols[:, :], cols_in[:, :]),
                             (eq[:, 0:SEQ], mask_in[:, :]), (posi[:, :], pos_in[:, :])):
                sp.dma_start(dst, src).then_inc(consts_in, 16)
            w_in_ = w_in.rearrange("(k p) n -> p k n", p=P)
            for c, (n, w) in enumerate(PROJ_CHUNKS):
                sp.dma_start(win_[c], w_in_[:, :, n:n + w]).then_inc(win_in[c], 16)
                if c == 0:
                    sp.dma_start(xt(1), x_in[P:SEQ, :]).then_inc(x_loaded[1], 16)
            sp.dma_start(uq, w_uq.rearrange("(k p) n -> p k n", p=P)).then_inc(uq_in, 16)
            sp.dma_start(ukv, w_ukv.rearrange("(k p) n -> p k n", p=P)).then_inc(ukv_in, 16)
            sp.dma_start(wout, w_out.rearrange("(k p) n -> p k n", p=P)).then_inc(wout_in, 16)

            def load_gain(p):
                n = min(p // TILES, LAYERS)
                sp.dma_start(xn[p % 2], gains_in[n:n + 1, :].to_broadcast([P, D])).then_inc(gain_in[p % 2], 16)

            def load_head(layer, h):
                sp.dma_start(wq_, wq_in[layer].rearrange("(k p) n -> p k n", p=P)[:, :, bass.ds(h * 2 * HALF, 2 * HALF)])\
                  .then_inc(wq_loaded, 16)
                sp.dma_start(skT[:, :], sk_in[layer][:, bass.ds(h * 2 * KEYS, 2 * KEYS)]).then_inc(wq_loaded, 16)

            load_gain(0)
            load_head(0, 0)
            for p in range(PHASES):
                if p == 0:
                    sp.wait_ge(x_mixed, 1)
                else:
                    sp.wait_ge(y_taken, p)
                load_gain(p + 1)
                with sp.Fori(1, HEADS) as h:
                    sp.wait_ge(s_ready, h + p * HEADS)
                    load_head(p // TILES, h)
                if p + 1 < PHASES:
                    sp.wait_ge(s_ready, (p + 1) * HEADS)
                    load_head((p + 1) // TILES, 0)
                if p == 0:
                    sp.wait_ge(x_mixed, TILES)
                    cw = c_in.rearrange("(k p) n -> p k n", p=P)
                    for j in range(4):
                        for g in range(2):
                            sp.dma_start(cin[:, j, :, g * 256:(g + 1) * 256], cw[:, :, g * D + j * 256:g * D + (j + 1) * 256])\
                              .then_inc(cin_in[j], 16)
                    load_conv_out(sp, 0)
            for t in range(TILES):
                sp.wait_ge(final_ready, t + 1)
                sp.dma_start(out[t * P:(t + 1) * P, :], xt(t)).then_inc(out_sent, 16)
            sp.wait_ge(out_sent, 16 * TILES)

        @block.gpsimd
        def _(pool):
            pool.sem_inc(ring_free, RING)
            for p in range(PHASES):
                with pool.Fori(0, HEADS) as h:
                    for k in range(TOPK):
                        if k % RING == 0:
                            pool.wait_ge(routed[k // RING], h + (p * HEADS + 1))
                        b = k % RING
                        pool.wait_ge(ring_free, h * TOPK + (p * SLOTS + k + 1))
                        settle(pool)
                        pool.indirect_dma_start(
                            out=ring[:, b * 2 * D:(b + 1) * 2 * D], out_offset=None, in_=table[:, :],
                            in_offset=bass.IndirectOffsetOnAxis(ap=idx[k // RING][:, b:b + 1], axis=0)).then_inc(row_in[b], 16)

        @block.tensor
        def _(pe):
            def mm(o_, l, r, start, stop, **kw):
                return nc.tensor.matmul(o_, l, r, start=start, stop=stop, **kw)

            def transposes(j, srcs, rows_=P):
                bank = bank_of(pe, j)
                for i, s in enumerate(srcs):
                    last = nc.tensor.transpose(bank[0:rows_, i * P:(i + 1) * P], s, ident[:, :])
                last.then_inc(bank_full[j % BANKS], 1)

            def turn_over(j, src):
                for i in range(2):
                    transposes(j + i, [src[:, (4 * i + k) * P:(4 * i + k + 1) * P] for k in range(4)])

            def gemm(j, lhs, rhs, width):
                bank = bank_of(pe, j)
                for k, (l, r) in enumerate(zip(lhs, rhs)):
                    last = mm(bank[:, 0:width], l, r, k == 0, k == len(lhs) - 1)
                last.then_inc(bank_full[j % BANKS], 1)

            def project(t):
                J = PROJ_AT[t]
                pe.wait_ge(hn_ready, t + 1)
                turn_over(J, o)
                emptied(pe, J)
                emptied(pe, J + 1)
                for c, (n, w) in enumerate(PROJ_CHUNKS):
                    if t == 0:
                        pe.wait_ge(win_in[c], 16)
                    gemm(J + 2 + c, [hT_[:, k, :] for k in range(KD)], [win_[c][:, k, :] for k in range(KD)], w)

            def mix_products(t):
                J = MIX_AT[t]
                pe.wait_ge(cn_ready, t + 1)
                transposes(J + J_C, [proj[t][:, i * P:(i + 1) * P] for i in range(3)])
                transposes(J + J_C + 1, [proj[t][:, OFF_KV + i * P:OFF_KV + (i + 1) * P] for i in range(2)])
                emptied(pe, J + J_C)
                pe.wait_ge(uq_in, 16)
                for i, w in enumerate((CHUNK, NQ - CHUNK)):
                    gemm(J + J_U + i, [cT[:, k, :] for k in range(3)],
                         [uq[:, k, i * CHUNK:i * CHUNK + w] for k in range(3)], w)
                emptied(pe, J + J_C + 1)
                pe.wait_ge(ukv_in, 16)
                for i in range(2):
                    gemm(J + J_KV + i, [cT[:, 3 + k, :] for k in range(2)],
                         [ukv[:, k, i * CHUNK:(i + 1) * CHUNK] for k in range(2)], CHUNK)
                pe.wait_ge(qpe_ready, t + 1)
                for i in range(2):
                    transposes(J + J_QT + i, [qsb[:, (4 * i + h) * QK:(4 * i + h + 1) * QK] for h in range(4)], QK)
                emptied(pe, J + J_KV)
                for i in range(2):
                    transposes(J + J_KT + i, [kfull[:, 4 * i + h, :] for h in range(4)], QK)
                pe.wait_ge(rope_ready, t + 1)
                transposes(J + J_MQT, [proj[t][:, OFF_MQ + i * P:OFF_MQ + (i + 1) * P] for i in range(4)])
                transposes(J + J_MKT, [proj[t][:, OFF_MK + i * P:OFF_MK + (i + 1) * P] for i in range(4)])

            def mix_heads(t, a0, a1):
                J = MIX_AT[t] + J_HEAD
                W = (t + 1) * P

                def scores(a):
                    j = J + 3 * a
                    bank = bank_of(pe, j)
                    mm(bank[:, 0:W], ident16[:, :], mask16[:, SEQ - W:SEQ], True, False)
                    if a < HEADS:
                        l, r = qT[0:QK, a, :], kT[0:QK, a, 0:W]
                    else:
                        b, s = (a - HEADS) // 2, HD * (a % 2)
                        l, r = mqT[s:s + HD, b, :], mkT[s:s + HD, b, 0:W]
                    mm(bank[:, 0:W], l, r, False, True).then_inc(bank_full[j % BANKS], 1)

                def values(a, s):
                    return vmla[s][:, a * VD:(a + 1) * VD] if a < HEADS else \
                        proj[s][:, OFF_MV + (a - HEADS) * HD:OFF_MV + (a - HEADS + 1) * HD]

                if a0 == 0:
                    for i in range(MIX_AT[t] + J_QT, MIX_AT[t] + J_HEAD):
                        emptied(pe, i)
                scores(a0)
                for a in range(a0, a1):
                    emptied(pe, J + 3 * a)
                    transposes(J + 3 * a + 1, [pb[a % 2][:, s * P:(s + 1) * P] for s in range(t + 1)])
                    if a + 1 < a1:
                        scores(a + 1)
                    emptied(pe, J + 3 * a + 1)
                    gemm(J + 3 * a + 2, [pT[a % 2][:, s, :] for s in range(t + 1)], [values(a, s) for s in range(t + 1)], VD)

            def mix_out(t):
                J = MIX_AT[t]
                pe.wait_ge(o_ready, t + 1)
                turn_over(J + J_OT, o)
                emptied(pe, J + J_OT)
                emptied(pe, J + J_OT + 1)
                pe.wait_ge(wout_in, 16)
                for i in range(2):
                    gemm(J + J_W + i, [hT_[:, k, :] for k in range(KD)],
                         [wout[:, k, i * CHUNK:(i + 1) * CHUNK] for k in range(KD)], CHUNK)

            def conv_glu(t, c0, c1):
                J = CONV_AT[t]
                if c0 == 0:
                    pe.wait_ge(hn_ready, TILES + t + 1)
                    turn_over(J, v)
                    emptied(pe, J)
                    emptied(pe, J + 1)
                for c in range(c0, c1):
                    if t == 0 and c % 2 == 0:
                        pe.wait_ge(cin_in[c // 2], 32)
                    j = J + J_GLU + c
                    bank = bank_of(pe, j)
                    for g in range(2):
                        cs = g * 256 + (c % 2) * P
                        for k in range(KD):
                            last = mm(bank[:, g * P:(g + 1) * P], cin[:, c // 2, k, cs:cs + P], hT_[:, k, :], k == 0, k == KD - 1)
                    last.then_inc(bank_full[j % BANKS], 1)

            def conv_norm(t):
                J = CONV_AT[t]
                pe.wait_ge(acc_ready, t + 1)
                turn_over(J + J_ACC, part["acc"])
                pe.wait_ge(z_ready, t + 1)
                turn_over(J + J_Z, v)
                emptied(pe, J + J_Z)
                emptied(pe, J + J_Z + 1)

            def conv_out(t, i):
                pe.wait_ge(cout_in, 32 * (2 * t + i + 1))
                gemm(CONV_AT[t] + J_CW + i, [hT_[:, k, :] for k in range(KD)], [cout[:, k, :] for k in range(KD)], CHUNK)

            def peer_q(H):
                pe.wait_ge(wq_loaded, (H + 1) * 32)
                held(pe, q_copied, H)
                for k in range(KD):
                    last = mm(qpsum[:, 0:2 * HALF], xnT[:, k, :], wq_[:, k, :], k == 0, k == KD - 1)
                last.then_inc(q_ready, 1)

            def peer_qT(H):
                pe.wait_ge(q_copied, H + 1)
                held(pe, qT_copied, H)
                for c in range(2):
                    last = nc.tensor.transpose(tpsum[:, c * P:(c + 1) * P], q_t[:, c * HALF:(c + 1) * HALF], ident[:, :])
                last.then_inc(qT_ready, 1)

            def peer_scores(H):
                pe.wait_ge(qT_copied, H + 1)
                held(pe, s_copied, H)
                for c in range(2):
                    last = mm(spsum[:, c * KEYS:(c + 1) * KEYS], q_T[:, c * P:(c + 1) * P], skT[:, c * KEYS:(c + 1) * KEYS], True, True)
                last.then_inc(s_ready, 1)

            def peer_slot(H, k, stop=False):
                pe.wait_ge(diag_ready, H * TOPK + (k + 1))
                b = k % RING
                for half in range(2):
                    last = mm(ypsum[:, half * CHUNK:(half + 1) * CHUNK], diag[:, (k % 2) * P:(k % 2 + 1) * P],
                              ring[:, b * 2 * D + D + half * CHUNK:b * 2 * D + D + (half + 1) * CHUNK], False, stop,
                              skip_group_check=True)
                last.then_inc(ring_free, 1)

            def peer_start(p):
                pe.wait_ge(xn_ready, p + 1)
                turn_over(NORM_AT[p], xn[p % 2])
                emptied(pe, NORM_AT[p])
                emptied(pe, NORM_AT[p] + 1)

            def peer_seed(p):
                if p:
                    pe.wait_ge(y_taken, p)
                for half in range(2):
                    mm(ypsum[:, half * CHUNK:(half + 1) * CHUNK], ident[:, :],
                       xt(p % TILES)[:, half * CHUNK:(half + 1) * CHUNK], True, False, skip_group_check=True)

            def peer_head(H, N, stop=False):
                for k in range(TOPK):
                    peer_slot(H, k, stop=stop and k == TOPK - 1)
                    if N is not None and k == 1:
                        peer_q(N)
                    if N is not None and k == 3:
                        peer_qT(N)
                    if N is not None and k == 5:
                        peer_scores(N)

            def heads(p, h0, h1):
                with pe.Fori(h0, h1) as h:
                    peer_head(h + p * HEADS, h + (p * HEADS + 1))

            def last_head(p):
                N = (p + 1) * HEADS
                peer_head(N - 1, N if p + 1 < PHASES else None, stop=True)
                if p + 1 < PHASES:
                    peer_seed(p + 1)

            pe.wait_ge(consts_in, 6 * 16)
            pe.wait_ge(id_ready, 1)
            project(0)
            project(1)
            mix_products(0)
            mix_heads(0, 0, ATTN_HEADS)
            mix_out(0)
            peer_start(0)
            peer_seed(0)
            peer_q(0)
            peer_qT(0)
            peer_scores(0)
            heads(0, 0, 1)
            mix_products(1)
            heads(0, 1, 2)
            mix_heads(1, 0, 8)
            heads(0, 2, 4)
            mix_heads(1, 8, 16)
            heads(0, 4, 5)
            mix_out(1)
            heads(0, 5, 7)
            peer_start(1)
            last_head(0)
            for p in (1, 2):
                heads(p, 0, 1)
                conv_glu(p - 1, 0, 4)
                heads(p, 1, 2)
                conv_glu(p - 1, 4, 8)
                heads(p, 2, 5)
                conv_norm(p - 1)
                conv_out(p - 1, 0)
                heads(p, 5, 6)
                conv_out(p - 1, 1)
                heads(p, 6, 7)
                peer_start(p + 1)
                last_head(p)
            heads(3, 0, 7)
            last_head(3)

        @block.scalar
        def _(act):
            own = Own(act, act_step)

            def run(out_, in_, func=ACT.Copy, **kw):
                return nc.scalar.activation(out_, in_, func, **kw)

            def free(j, ins):
                ins.then_inc(bank_free[j % BANKS], 1)

            def take(j, out_, n=CHUNK, rows_=P, **kw):
                full(act, j)
                free(j, run(out_, banks[j % BANKS][0:rows_, 0:n], **kw))

            def take_scaled(j, dst, k0, count, col):
                full(act, j)
                for i in range(count):
                    last = run(dst[:, k0 + i, :], banks[j % BANKS][:, i * P:(i + 1) * P], scale=cols[:, col + i:col + i + 1])
                free(j, last)

            def project(t):
                J = PROJ_AT[t]
                for i in range(2):
                    take_scaled(J + i, hT_, 4 * i, 4, C_MIX + 4 * i)
                for c, (n, w) in enumerate(PROJ_CHUNKS):
                    take(J + 2 + c, proj[t][:, n:n + w], w)

            def mix_products(t):
                J = MIX_AT[t]
                if t:
                    act.wait_ge(x_mixed, t)
                take_scaled(J + J_C, cT, 0, 3, C_QN)
                take_scaled(J + J_C + 1, cT, 3, 2, C_KVN)
                take(J + J_U, qsb[:, 0:CHUNK])
                take(J + J_U + 1, qsb[:, CHUNK:NQ], NQ - CHUNK)
                full(act, J + J_KV)
                free(J + J_KV, run(kfull[:, :, 0:NOPE], banks[(J + J_KV) % BANKS][:, :].rearrange("p (h d) -> p h d", h=HEADS)))
                take(J + J_KV + 1, vmla[t])
                for i in range(2):
                    take(J + J_QT + i, qT[0:QK, 4 * i:4 * i + 4, :].rearrange("p h t -> p (h t)"), rows_=QK, scale=QK ** -0.5)

                def keys(j, dst, rows_):
                    full(act, j)
                    free(j, run(dst, banks[j % BANKS][0:rows_, :].rearrange("p (h t) -> p h t", h=4)))
                for i in range(2):
                    keys(J + J_KT + i, kT[0:QK, 4 * i:4 * i + 4, t * P:(t + 1) * P], QK)
                take(J + J_MQT, mqT[:, :, :].rearrange("p h t -> p (h t)"), scale=HD ** -0.5)
                keys(J + J_MKT, mkT[:, :, t * P:(t + 1) * P], P)

            def mix_heads(t, a0, a1):
                J = MIX_AT[t] + J_HEAD
                W = (t + 1) * P
                for a in range(a0, a1):
                    act.wait_ge(max_ready, t * ATTN_HEADS + a + 1)
                    if a >= 2:
                        emptied(act, J + 3 * (a - 2) + 1)
                    free(J + 3 * a, run(pb[a % 2][:, 0:W], banks[(J + 3 * a) % BANKS][:, 0:W], ACT.Exp,
                                        bias=nmax[:, a % 2:a % 2 + 1], accum_out=rows[:, a:a + 1]))

            def mix_out(t):
                J = MIX_AT[t] + J_OT
                for i in range(2):
                    take(J + i, hT[:, i * CHUNK:(i + 1) * CHUNK])

            def conv_glu(t, c0, c1):
                J = CONV_AT[t]
                if t and c0 == 0:
                    act.wait_ge(half_done, 2 * t)
                if c0 == 0:
                    for i in range(2):
                        take_scaled(J + i, hT_, 4 * i, 4, C_MIX + KD + 4 * i)
                for c in range(c0, c1):
                    j = J + J_GLU + c
                    full(act, j)
                    if c >= 2:
                        emptied(act, j - 2)
                    run(sig[c % 2], banks[j % BANKS][:, P:2 * P], ACT.Sigmoid,
                        bias=cols[:, C_BIN + KD + c:C_BIN + KD + c + 1]).then_inc(sig_ready, 1)

            def conv_norm(t):
                J = CONV_AT[t]
                for i in range(2):
                    take(J + J_ACC + i, v[:, i * CHUNK:(i + 1) * CHUNK])
                for i in range(2):
                    j = J + J_Z + i
                    full(act, j)
                    for k in range(4):
                        c = 4 * i + k
                        last = run(hT_[:, c, :], banks[j % BANKS][:, k * P:(k + 1) * P], ACT.Silu,
                                   scale=cols[:, C_LNG + c:C_LNG + c + 1], bias=cols[:, C_LNB + c:C_LNB + c + 1])
                    free(j, last)

            def peer_copy(H, ready, copied, dst, psum, used):
                act.wait_ge(ready, H + 1)
                held(act, used, H)
                if dst is q_t:
                    held(act, routed[0], H)
                run(dst[:, :], psum[:, 0:2 * P]).then_inc(copied, 1)

            def peer_exp(H):
                act.wait_ge(best_ready, H + 1)
                run(e_g[:, :], best[:, :], ACT.Exp, bias=nbest[:, 0:1], accum_out=e_sum[:, 0:1]).then_inc(exp_ready, 1)

            def peer_gates(H):
                act.wait_ge(g_ready, H + 1)
                run(g_cur[:, :], g_next[:, :]).then_inc(g_taken, 1)
                act.wait_ge(g_taken, H + 1)

            def peer_slot(H, k, first=False):
                act.wait_ge(dot_ready, H * TOPK + (k + 1))
                own.then(run(gel[:, k:k + 1], dot[:, k:k + 1], ACT.Gelu))
                own.then(run(coef[:, k:k + 1], gel[:, k:k + 1], scale=g_cur[:, k:k + 1]))
                if not (first and k < 2):
                    act.wait_ge(ring_free, H * TOPK + (k - 1 + RING))
                run(diag[:, (k % 2) * P:(k % 2 + 1) * P], ident[:, :], scale=coef[:, k:k + 1]).then_inc(diag_ready, 1)

            def peer_start(p):
                for i in range(2):
                    take(NORM_AT[p] + i, xnT_[:, i * CHUNK:(i + 1) * CHUNK])

            def peer_head(H, N):
                peer_gates(H)
                for k in range(TOPK):
                    peer_slot(H, k)
                    if N is not None and k == 1:
                        peer_copy(N, q_ready, q_copied, q_t, qpsum, qT_ready)
                    if N is not None and k == 3:
                        peer_copy(N, qT_ready, qT_copied, q_T, tpsum, s_ready)
                    if N is not None and k == 5:
                        peer_copy(N, s_ready, s_copied, sc, spsum, routed[0])
                    if N is not None and k == 9:
                        peer_exp(N)

            def heads(p, h0, h1):
                with act.Fori(h0, h1) as h:
                    with own.loop(h - h0, h1 - h0, 2 * TOPK):
                        peer_head(h + p * HEADS, h + (p * HEADS + 1))

            def last_head(p):
                N = (p + 1) * HEADS
                peer_head(N - 1, N if p + 1 < PHASES else None)

            act.wait_ge(consts_in, 6 * 16)
            act.wait_ge(id_ready, 2)
            run(trig[:, :], trig[:, :], ACT.Sin).then_inc(id_ready, 1)
            project(0)
            project(1)
            mix_products(0)
            mix_heads(0, 0, ATTN_HEADS)
            mix_out(0)
            peer_start(0)
            peer_copy(0, q_ready, q_copied, q_t, qpsum, qT_ready)
            peer_copy(0, qT_ready, qT_copied, q_T, tpsum, s_ready)
            peer_copy(0, s_ready, s_copied, sc, spsum, routed[0])
            peer_exp(0)
            heads(0, 0, 1)
            mix_products(1)
            heads(0, 1, 2)
            mix_heads(1, 0, 8)
            heads(0, 2, 4)
            mix_heads(1, 8, 16)
            heads(0, 4, 5)
            mix_out(1)
            heads(0, 5, 7)
            peer_start(1)
            last_head(0)
            for p in (1, 2):
                heads(p, 0, 1)
                conv_glu(p - 1, 0, 4)
                heads(p, 1, 2)
                conv_glu(p - 1, 4, 8)
                heads(p, 2, 5)
                conv_norm(p - 1)
                load_conv_out(act, 2 * p - 1)
                heads(p, 5, 6)
                if p == 1:
                    load_conv_out(act, 2)
                heads(p, 6, 7)
                peer_start(p + 1)
                last_head(p)
            heads(3, 0, 7)
            last_head(3)

        @block.vector
        def _(dve):
            own = Own(dve, dve_step)
            V = nc.vector

            def free(j, ins):
                ins.then_inc(bank_free[j % BANKS], 1)

            def power(var, w, y, tmp):
                yi, vi = y.bitcast(i32), var.bitcast(i32)
                own.then(V.tensor_scalar(smalli[:, 0:w], vi, 1, None, ALU.logical_shift_right))
                own.then(V.tensor_scalar(yi, smalli[:, 0:w], -1.0, float(0x5f3759df), ALU.mult, ALU.add))
                for _ in range(4):
                    own.then(V.tensor_tensor(tmp, y, y, ALU.mult))
                    own.then(V.tensor_tensor(tmp, tmp, var, ALU.mult))
                    own.then(V.tensor_scalar(tmp, tmp, -0.5, 1.5, ALU.mult, ALU.add))
                    own.then(V.tensor_tensor(y, y, tmp, ALU.mult))

            def mean_square(src, n, c):
                own.then(V.tensor_tensor_reduce(out=junk[:, 0:n], in0=src, in1=src, scale=1.0, scalar=0.0,
                                                op0=ALU.mult, op1=ALU.add, accum_out=small[:, c:c + 1]))
                own.then(V.tensor_scalar(small[:, c:c + 1], small[:, c:c + 1], 1.0 / n, EPS, ALU.mult, ALU.add))

            def rms(src, n):
                mean_square(src, n, 0)
                power(small[:, 0:1], 1, small[:, 2:3], small[:, 4:5])
                return small[:, 2:3]

            def project(t):
                dve.wait_ge(x_loaded[t], 16)
                r = rms(xt(t), D)
                if t:
                    emptied(dve, PROJ_AT[t - 1] + 1)
                V.tensor_scalar(o, xt(t), r, None, ALU.mult).then_inc(hn_ready, 1)

            def rotate(src, heads, half, t, f0):
                c = trig[:, t * 2 * NF + f0:t * 2 * NF + f0 + half].unsqueeze(1).to_broadcast([P, heads, half])
                s = trig[:, t * 2 * NF + NF + f0:t * 2 * NF + NF + f0 + half].unsqueeze(1).to_broadcast([P, heads, half])
                x1, x2 = src[:, :, 0:half], src[:, :, half:2 * half]
                a, b = (r[:, 0:heads * half].rearrange("p (h d) -> p h d", h=heads) for r in rtmp)
                own.did(V.tensor_tensor(a, x1, s, ALU.mult))
                own.then(V.tensor_tensor(b, x2, s, ALU.mult))
                own.did(V.tensor_tensor(x1, x1, c, ALU.mult))
                own.then(V.tensor_tensor(x2, x2, c, ALU.mult))
                own.did(V.tensor_tensor(x1, x1, b, ALU.subtract))
                own.then(V.tensor_tensor(x2, x2, a, ALU.add))

            def mix_products(t):
                J = MIX_AT[t]
                for c in range(len(PROJ_CHUNKS)):
                    emptied(dve, PROJ_AT[t] + 2 + c)
                mean_square(proj[t][:, 0:Q_LORA], Q_LORA, 0)
                mean_square(proj[t][:, OFF_KV:OFF_ROPE], KV_LORA, 1)
                power(small[:, 0:2], 2, small[:, 2:4], small[:, 4:6])
                V.tensor_scalar(proj[t][:, 0:Q_LORA], proj[t][:, 0:Q_LORA], small[:, 2:3], None, ALU.mult)
                V.tensor_scalar(proj[t][:, OFF_KV:OFF_ROPE], proj[t][:, OFF_KV:OFF_ROPE], small[:, 3:4], None, ALU.mult)\
                 .then_inc(cn_ready, 1)
                dve.wait_ge(id_ready, 3)
                if t == 0:
                    emptied(dve, PROJ_AT[1] + 1)
                rotate(proj[t][:, OFF_ROPE:OFF_MQ].unsqueeze(1), 1, ROPE // 2, t, 0)
                own.did(V.tensor_copy(kfull[:, :, NOPE:QK], proj[t][:, OFF_ROPE:OFF_MQ].unsqueeze(1).to_broadcast([P, HEADS, ROPE])))
                for off in (OFF_MQ, OFF_MK):
                    rotate(proj[t][:, off:off + MOBA].rearrange("p (h d) -> p h d", h=HEADS), HEADS, HD // 2, t, ROPE // 2)
                dve.sem_inc(rope_ready, 1)
                for i in range(2):
                    emptied(dve, J + J_U + i)
                rotate(qsb.rearrange("p (h d) -> p h d", h=HEADS)[:, :, NOPE:QK], HEADS, ROPE // 2, t, 0)
                dve.sem_inc(qpe_ready, 1)

            def mix_heads(t, a0, a1):
                J = MIX_AT[t] + J_HEAD
                W = (t + 1) * P

                def maximum(a):
                    j = J + 3 * a
                    full(dve, j)
                    V.tensor_reduce(nmax[:, a % 2:a % 2 + 1], banks[j % BANKS][:, 0:W], AX.X, ALU.max, negate=True)\
                     .then_inc(max_ready, 1)

                maximum(a0)
                for a in range(a0, a1):
                    j = J + 3 * a + 1
                    full(dve, j)
                    if a == 0:
                        emptied(dve, MIX_AT[t] + J_KT + 1)
                    free(j, V.tensor_copy(pT[a % 2][:, 0:t + 1, :].rearrange("p s t -> p (s t)"), banks[j % BANKS][:, 0:W]))
                    if a + 1 < a1:
                        maximum(a + 1)
                    own.then(V.reciprocal(rinv[:, a:a + 1], rows[:, a:a + 1]))
                    full(dve, j + 1)
                    ins = V.tensor_scalar(o[:, a * VD:(a + 1) * VD], banks[(j + 1) % BANKS][:, 0:VD], rinv[:, a:a + 1], None, ALU.mult)
                    free(j + 1, ins)
                if a1 == ATTN_HEADS:
                    emptied(dve, J + 3 * (ATTN_HEADS - 1) + 2)
                    dve.sem_inc(o_ready, 1)

            def mix_out(t):
                for i in range(2):
                    j = MIX_AT[t] + J_W + i
                    full(dve, j)
                    xs = xt(t)[:, i * CHUNK:(i + 1) * CHUNK]
                    free(j, V.tensor_tensor(xs, xs, banks[j % BANKS][:, :], ALU.add))
                for i in range(2):
                    emptied(dve, MIX_AT[t] + J_W + i)
                dve.sem_inc(x_mixed, 1)

            def conv_glu(t, c0, c1):
                J = CONV_AT[t]
                if c0 == 0:
                    r = rms(xt(t), D)
                    V.tensor_scalar(v, xt(t), r, None, ALU.mult).then_inc(hn_ready, 1)
                    if t == 0:
                        own.did(V.memset(uT[:, :, 0:TAPS - 1], 0.0))
                for c in range(c0, c1):
                    j = J + J_GLU + c
                    dve.wait_ge(sig_ready, t * KD + c + 1)
                    full(dve, j)
                    free(j, V.scalar_tensor_tensor(out=uT[:, c, TAPS - 1 + t * P:TAPS - 1 + (t + 1) * P],
                                                   in0=banks[j % BANKS][:, 0:P], scalar=cols[:, C_BIN + c:C_BIN + c + 1],
                                                   in1=sig[c % 2], op0=ALU.add, op1=ALU.mult))

            def first_tap(t):
                for c in range(KD):
                    emptied(dve, CONV_AT[t] + J_GLU + c)
                for c in range(KD):
                    own.did(V.tensor_scalar(acc[:, c, :], uT[:, c, t * P:(t + 1) * P], cols[:, C_TAPS + c * TAPS:C_TAPS + c * TAPS + 1],
                                            cols[:, C_BDW + c:C_BDW + c + 1], ALU.mult, ALU.add))

            def tap(t, k):
                for c in range(KD):
                    own.wait(KD - 1)
                    own.did(V.scalar_tensor_tensor(
                        out=acc[:, c, :], in0=uT[:, c, bass.ds(k + t * P, P)],
                        scalar=cols[:, bass.ds(k + (C_TAPS + c * TAPS), 1)], in1=acc[:, c, :], op0=ALU.mult, op1=ALU.add))

            def taps_done():
                own.wait()
                dve.sem_inc(acc_ready, 1)

            def conv_norm(t):
                J = CONV_AT[t]
                for i in range(2):
                    emptied(dve, J + J_ACC + i)
                    own.did(V.bn_stats(small[:, 0:6] if i == 0 else eqs, v[:, i * CHUNK:(i + 1) * CHUNK]))
                own.wait()
                own.then(V.bn_aggr(small[:, 12:14], small[:, 0:12]))
                own.then(V.tensor_scalar(small[:, 0:1], small[:, 13:14], EPS, None, ALU.add))
                power(small[:, 0:1], 1, small[:, 2:3], small[:, 4:5])
                V.tensor_scalar(v, v, small[:, 12:13], small[:, 2:3], ALU.subtract, ALU.mult).then_inc(z_ready, 1)

            eqs = small[:, 6:12]

            def conv_out(t, i):
                j = CONV_AT[t] + J_CW + i
                full(dve, j)
                xs = xt(t)[:, i * CHUNK:(i + 1) * CHUNK]
                free(j, V.tensor_tensor(xs, xs, banks[j % BANKS][:, :], ALU.add))
                emptied(dve, j)
                V.tensor_tensor(xs, xs, cbias, ALU.add).then_inc(half_done, 1)
                dve.wait_ge(half_done, 2 * t + i + 1)

            def route(H, layer, part_):
                top_, topi_, topf_ = (r[:, :].rearrange("p (c k) -> p c k", c=2) for r in (top, topi, topf))
                sc_, sc2_ = (r[:, :].rearrange("p (c k) -> p c k", c=2) for r in (sc, sc2))
                low = -3.0e38
                if part_ == 0:
                    dve.wait_ge(s_copied, H + 1)
                    settle(dve)
                    for c in range(2):
                        own.did(V.max(top_[:, c, 0:8], sc_[:, c, :]))
                    for c in range(2):
                        own.wait(1)
                        settle(dve)
                        own.did(V.max_index(topi_[:, c, 0:8], top_[:, c, 0:8], sc_[:, c, :]))
                        own.did(V.match_replace(sc2_[:, c, :], top_[:, c, 0:8], sc_[:, c, :], low))
                    own.wait()
                if part_ == 1:
                    settle(dve)
                    for c in range(2):
                        own.did(V.max(top_[:, c, 8:16], sc2_[:, c, :]))
                    for c in range(2):
                        own.wait(1)
                        settle(dve)
                        own.did(V.max_index(topi_[:, c, 8:16], top_[:, c, 8:16], sc2_[:, c, :]))
                    own.wait()
                    own.did(V.tensor_scalar(topf_[:, 0, :], topi_[:, 0, :], float(layer * KEYS), None, ALU.add))
                    own.did(V.tensor_copy(topf_[:, 1, :], topi_[:, 1, :]))
                cand, cand2 = sc2, sc
                if part_ == 2:
                    own.then(V.tensor_tensor(cand[:, :].rearrange("p (a b) -> p a b", a=TOPK),
                                             top_[:, 0, :].unsqueeze(2).to_broadcast([P, TOPK, TOPK]),
                                             top_[:, 1, :].unsqueeze(1).to_broadcast([P, TOPK, TOPK]), ALU.add))
                    settle(dve)
                    own.then(V.max(best[:, 0:8], cand[:, :]))
                    settle(dve)
                    own.did(V.max_index(pos[:, 0:8], best[:, 0:8], cand[:, :]))
                    own.then(V.match_replace(cand2[:, :], best[:, 0:8], cand[:, :], low))
                if part_ == 3:
                    settle(dve)
                    own.then(V.max(best[:, 8:16], cand2[:, :]))
                    settle(dve)
                    own.did(V.max_index(pos[:, 8:16], best[:, 8:16], cand2[:, :]))
                    V.tensor_scalar(nbest[:, :], best[:, 0:1], -1.0, None, ALU.mult).then_inc(best_ready, 1)
                    own.wait()
                    own.did(V.tensor_scalar(pos2[:, 0:TOPK], pos[:, :], 4, None, ALU.logical_shift_right))
                    own.then(V.tensor_scalar(pos2[:, TOPK:2 * TOPK], pos[:, :], TOPK - 1, None, ALU.bitwise_and))
                eq_ = eq[:, :].rearrange("p (c k a) -> p (c k) a", c=2, k=TOPK)
                eq4 = eq[:, :].rearrange("p (c k a) -> p c k a", c=2, k=TOPK)
                if part_ == 4:
                    own.then(V.tensor_tensor(eq_, pos2[:, :].unsqueeze(2).to_broadcast([P, 2 * TOPK, TOPK]),
                                             iota16[:, :].unsqueeze(1).to_broadcast([P, 2 * TOPK, TOPK]), ALU.is_equal))
                    own.then(V.tensor_tensor(eq4, eq4, topf_.unsqueeze(2).to_broadcast([P, 2, TOPK, TOPK]), ALU.mult))
                    own.then(V.tensor_reduce(sel[:, :], eq_, AX.X, ALU.add))
                if part_ in (5, 7):
                    i = (part_ - 5) // 2
                    V.scalar_tensor_tensor(out=idx[i][:, :], in0=sel[:, i * RING:(i + 1) * RING], scalar=float(KEYS),
                                           in1=sel[:, TOPK + i * RING:TOPK + (i + 1) * RING],
                                           op0=ALU.mult, op1=ALU.add).then_inc(routed[i], 1)
                if part_ == 6:
                    dve.wait_ge(exp_ready, H + 1)
                    own.then(V.reciprocal(e_inv[:, :], e_sum[:, :]))
                    held(dve, g_taken, H)
                    V.tensor_scalar(g_next[:, :], e_g[:, :], e_inv[:, :], None, ALU.mult).then_inc(g_ready, 1)

            OWN_PER_ROUTE = 6 + 6 + 4 + 4 + 3 + 1

            def dots(p, H, k):
                b = k % RING
                dve.wait_ge(row_in[b], H * 32 + 16 * (k // RING + 1))
                V.tensor_tensor_reduce(out=junk[:, :], in0=xn[p % 2], in1=ring[:, b * 2 * D:b * 2 * D + D], scale=1.0, scalar=0.0,
                                       op0=ALU.mult, op1=ALU.add, accum_out=dot[:, k:k + 1]).then_inc(dot_ready, 1)
                dve.wait_ge(dot_ready, H * TOPK + (k + 1))

            def peer_start(p):
                r = rms(xt(p % TILES), D)
                dve.wait_ge(gain_in[p % 2], 16 * (p // 2 + 1))
                V.scalar_tensor_tensor(out=xn[p % 2], in0=xt(p % TILES), scalar=r, in1=xn[p % 2], op0=ALU.mult, op1=ALU.mult)\
                 .then_inc(xn_ready, 1)
                dve.wait_ge(xn_ready, p + 1)

            TAP_SLOTS = [0, 1, 2, 3, 4, 5, 12, 13, 14, 15]

            def peer_head(p, H, N, layer, first_of=None):
                for k in range(TOPK):
                    dots(p, H, k)
                    if N is not None and 6 <= k < 13:
                        route(N, layer, k - 6)
                    if first_of is not None and k in TAP_SLOTS:
                        tap(p - 1, first_of + TAP_SLOTS.index(k))
                if N is not None:
                    route(N, layer, 7)

            def heads(p, h0, h1, taps=False):
                per = OWN_PER_ROUTE + (KD * len(TAP_SLOTS) if taps else 0)
                with dve.Fori(h0, h1) as h:
                    with own.loop(h - h0, h1 - h0, per):
                        peer_head(p, h + p * HEADS, h + (p * HEADS + 1), p // TILES, (h - h0) * len(TAP_SLOTS) + 1 if taps else None)

            def peer_end(p):
                dve.wait_ge(ring_free, RING + (p + 1) * SLOTS)
                V.tensor_copy(xt(p % TILES), ypsum[:, :]).then_inc(y_taken, 1)
                dve.wait_ge(y_taken, p + 1)

            def last_head(p):
                N = (p + 1) * HEADS
                peer_head(p, N - 1, N if p + 1 < PHASES else None, (p + 1) // TILES)
                peer_end(p)

            def final(t):
                r = rms(xt(t), D)
                dve.wait_ge(gain_in[PHASES % 2], 16 * (PHASES // 2 + 1))
                V.scalar_tensor_tensor(out=xt(t), in0=xt(t), scalar=r, in1=xn[PHASES % 2], op0=ALU.mult, op1=ALU.mult)\
                 .then_inc(final_ready, 1)

            dve.wait_ge(consts_in, 6 * 16)
            own.did(V.tensor_copy(mask16[:, :], eq[:, 0:SEQ]))
            V.tensor_copy(ident16[:, :], ident[:, :]).then_inc(id_ready, 1)
            own.then(V.tensor_copy(posf[:, :], posi[:, :]))
            C1 = 6.28125
            C2 = float(np.float32(np.int32(np.float64(2 * np.pi - C1) * 2 ** 20) / 2 ** 20))
            C3 = float(np.float32(2 * np.pi - C1 - C2))
            magic = 12582912.0
            turns, ang = eq[:, 256:256 + 2 * NF], eq[:, 384:384 + 2 * NF]
            for t in range(TILES):
                for c in range(2):
                    own.did(V.tensor_scalar(ang[:, c * NF:(c + 1) * NF], inv[:, :], posf[:, t:t + 1], None, ALU.mult))
                own.wait()
                for c, quarter in ((0, 0.25), (1, 0.0)):
                    s = slice(c * NF, (c + 1) * NF)
                    own.then(V.tensor_scalar(turns[:, s], ang[:, s], float(1 / (2 * np.pi)), quarter, ALU.mult, ALU.add))
                    own.then(V.tensor_scalar(turns[:, s], turns[:, s], magic, -magic, ALU.add, ALU.add))
                    for part_ in (C1, C2, C3):
                        own.then(V.scalar_tensor_tensor(out=ang[:, s], in0=turns[:, s], scalar=-part_, in1=ang[:, s], op0=ALU.mult, op1=ALU.add))
                    if c == 0:
                        own.then(V.tensor_scalar(ang[:, s], ang[:, s], float(np.pi / 2), None, ALU.add))
                own.then(V.tensor_scalar(trig[:, t * 2 * NF:(t + 1) * 2 * NF], ang, 3.1415925, -3.1415925, ALU.min, ALU.max))
            dve.sem_inc(id_ready, 1)
            project(0)
            project(1)
            mix_products(0)
            mix_heads(0, 0, ATTN_HEADS)
            mix_out(0)
            peer_start(0)
            for part_ in range(8):
                route(0, 0, part_)
            heads(0, 0, 1)
            mix_products(1)
            heads(0, 1, 2)
            mix_heads(1, 0, 8)
            heads(0, 2, 4)
            mix_heads(1, 8, 16)
            heads(0, 4, 5)
            mix_out(1)
            heads(0, 5, 7)
            peer_start(1)
            last_head(0)
            for p in (1, 2):
                heads(p, 0, 1)
                conv_glu(p - 1, 0, 4)
                heads(p, 1, 2)
                conv_glu(p - 1, 4, 8)
                first_tap(p - 1)
                heads(p, 2, 5, taps=True)
                taps_done()
                conv_norm(p - 1)
                conv_out(p - 1, 0)
                heads(p, 5, 6)
                conv_out(p - 1, 1)
                heads(p, 6, 7)
                peer_start(p + 1)
                last_head(p)
            heads(3, 0, 5)
            final(0)
            heads(3, 5, 7)
            last_head(3)
            final(1)


def kernel(**inputs):
    import concourse.bacc as bacc
    from concourse.bass_utils import run_bass_kernel_spmd

    a = {k: np.asarray(v) for k, v in inputs.items()}

    def split(w):
        return np.ascontiguousarray(w.reshape(-1, P).T)

    taps = a["conv_w_dw"][0].reshape(TAPS, KD, P).transpose(2, 1, 0).reshape(P, KD * TAPS)
    cols = np.concatenate([split(a["norm_mix"]), split(a["conv_b_in"]), split(a["conv_b_dw"]), split(a["conv_ln_g"]),
                           split(a["conv_ln_b"]), split(a["mla_q_norm"]), split(a["mla_kv_norm"]), taps], axis=1)
    f = np.float32
    inv = np.concatenate([f(1.0) / (f(THETA) ** (np.arange(0, d, 2, dtype=f) / f(d))) for d in (ROPE, HD)])
    const = np.concatenate([np.eye(P, dtype=f), np.tile(np.arange(TOPK, dtype=f), (P, 1)), np.tile(inv.astype(f), (P, 1))], axis=1)
    mask = np.concatenate([np.zeros((P, P), f), np.triu(np.full((P, P), -1e30, f), 1)], axis=1)
    ukv = a["mla_w_ukv"][0].reshape(KV_LORA, HEADS, 2, NOPE).transpose(0, 2, 1, 3).reshape(KV_LORA, D)
    arrays = {
        "x": a["x"].reshape(SEQ, D),
        "positions": np.ascontiguousarray(a["positions"].reshape(TILES, P).T),
        "cols": cols, "const": const, "mask": mask,
        "w_in": a["attn_w_in"][0], "w_uq": a["mla_w_uq"][0], "w_ukv": ukv, "w_out": a["attn_w_out"][0],
        "c_in": a["conv_w_in"][0], "c_out": a["conv_w_out"][0], "c_bout": a["conv_b_out"],
        "wq": a["peer_w_q"],
        "sk": a["peer_subkeys"].transpose(0, 4, 1, 2, 3).reshape(LAYERS, HALF, HEADS * 2 * KEYS),
        "gains": np.concatenate([a["norm_ffn"], a["norm_final"].reshape(1, D)], axis=0),
        "table": np.concatenate([a["peer_u"], a["peer_v"]], axis=2).reshape(LAYERS * EXPERTS, 2 * D),
    }
    arrays = {k: np.ascontiguousarray(v) for k, v in arrays.items()}
    nc = bacc.Bacc("TRN2", target_bir_lowering=False, num_devices=1)
    args = [nc.dram_tensor(f"{k}_dram", v.shape, mybir.dt.from_np(v.dtype), kind="ExternalInput").ap() for k, v in arrays.items()]
    out = nc.dram_tensor("out_dram", (SEQ, D), mybir.dt.float32, kind="ExternalOutput").ap()
    build(nc, *args, out)
    r = run_bass_kernel_spmd(nc, [{f"{k}_dram": v for k, v in arrays.items()}], core_ids=[0])
    return r.results[0]["out_dram"].reshape(1, SEQ, D)
```

```python
from contextlib import ExitStack, contextmanager

import numpy as np
import concourse.bass as bass
from concourse import mybir

P = 128
SEQ, D = 256, 1024
TILES = SEQ // P
KD = D // P
LAYERS = 2
EPS = 1e-6
THETA = 10000.0
HEADS = 8
Q_LORA, KV_LORA, NOPE, ROPE, VD = 384, 256, 64, 32, 64
QK = NOPE + ROPE
HD = 64
MOBA = HEADS * HD
OFF_KV, OFF_ROPE = Q_LORA, Q_LORA + KV_LORA
OFF_MQ = OFF_ROPE + ROPE
OFF_MK, OFF_MV = OFF_MQ + MOBA, OFF_MQ + 2 * MOBA
D_IN = OFF_MQ + 3 * MOBA
NQ = HEADS * QK
TAPS = 31
KEYS, TOPK, HALF = 128, 16, 128
EXPERTS = KEYS * KEYS
RING = 8
NF = ROPE // 2 + HD // 2
PHASES = LAYERS * TILES
SLOTS = HEADS * TOPK
CHUNK = 512
PROJ_CHUNKS = [(n, min(CHUNK, D_IN - n)) for n in range(0, D_IN, CHUNK)]
ATTN_HEADS = 2 * HEADS

C_MIX = 0
C_BIN = C_MIX + LAYERS * KD
C_BDW = C_BIN + 2 * KD
C_LNG = C_BDW + KD
C_LNB = C_LNG + KD
C_QN = C_LNB + KD
C_KVN = C_QN + Q_LORA // P
C_TAPS = C_KVN + KV_LORA // P
COLS = C_TAPS + KD * TAPS

K_ID, K_IOTA = 0, P
K_INV = K_IOTA + TOPK
KCOLS = K_INV + NF

N_PROJ, N_NORM = 2 + len(PROJ_CHUNKS), 2
J_C, J_U, J_KV, J_QT, J_KT, J_MQT, J_MKT, J_HEAD = 0, 2, 4, 6, 8, 10, 11, 12
J_OT = J_HEAD + 3 * ATTN_HEADS
J_W = J_OT + 2
N_MIX = J_W + 2
J_GLU, J_ACC, J_Z, J_CW = 2, 2 + KD, 4 + KD, 6 + KD
N_CONV = J_CW + 2
SECOND = 3000
PROJ_AT = [0, SECOND]
OUT_AT = SECOND + 4
MIX_AT = [N_PROJ, N_PROJ + J_OT + N_NORM + 2]
NORM_AT = [MIX_AT[0] + J_OT, MIX_AT[1] + N_MIX]
PROJ_JOB = [[2, 3, 4, 5, 6], [SECOND + 2, NORM_AT[0] + N_NORM, OUT_AT + KD, NORM_AT[0] + N_NORM + 1, SECOND + 3]]
WIN_AT = [0, 2, 1, 3]
CONV_AT = [NORM_AT[1] + N_NORM, NORM_AT[1] + 2 * N_NORM + N_CONV]
NORM_AT += [CONV_AT[0] + N_CONV, CONV_AT[1] + N_CONV]
BANKS = 3


def bank_no(j):
    return j % BANKS if j < SECOND else BANKS + (j - SECOND) % BANKS


def turn_no(j):
    return (j if j < SECOND else j - SECOND) // BANKS


HEAD_W = KD * 2 * HALF + 2 * KEYS
KEPT_FROM = 4
OUT_HEADS = [2, 4, 6, 8, 10, 12, 14]
HEAD_SLOT = 25
GLU_SLOTS = [7, 9, 11, 13, 21, 25, 29, 37]
TAPS_AT = [16, 46]
TAP_SLOTS = range(1, TOPK)


def build(nc, x_in, pos_in, cols_in, const_in, mask_in, w_in, w_uq, w_ukv, w_out, c_in, c_out, c_bout,
          heads_in, gains_in, table, out):
    f32, bf16, i32, u32 = mybir.dt.float32, mybir.dt.bfloat16, mybir.dt.int32, mybir.dt.uint32
    ALU, ACT, AX = mybir.AluOpType, mybir.ActivationFunctionType, mybir.AxisListType
    ctx = ExitStack()
    with ctx:
        def sb(name, words, dt=f32):
            return ctx.enter_context(nc.sbuf_tensor(name, [P, words], dt))

        def sem(name):
            return ctx.enter_context(nc.semaphore(name))

        ident = sb("ident", P)
        ident16 = sb("ident16", P, bf16)
        mask16 = sb("mask16", SEQ, bf16)
        iota16 = sb("iota16", TOPK)
        inv = sb("inv", NF)
        cols = sb("cols", COLS)
        trig = sb("trig", TILES * 2 * NF)
        x = sb("x", TILES * D)
        hT = sb("hT", D)
        xns = sb("xns", 3 * D)
        junk = sb("junk", D, bf16)
        head = sb("head", HEAD_W)
        ring = sb("ring", RING * 2 * D)

        def xt(t):
            return x[:, t * D:(t + 1) * D]

        xn = [xns[:, 0:D], xns[:, 2 * D:3 * D]]
        xnT_ = xns[:, D:2 * D]
        xnT = xnT_.rearrange("p (k t) -> p k t", k=KD)
        hT_ = hT[:, :].rearrange("p (k t) -> p k t", k=KD)
        wq_, skT = head[:, 0:KD * 2 * HALF].rearrange("p (k n) -> p k n", k=KD), head[:, KD * 2 * HALF:HEAD_W]
        win_ = [ring[:, WIN_AT[n // w] * w * KD:(WIN_AT[n // w] + 1) * w * KD].rearrange("p (k n) -> p k n", k=KD) if w == CHUNK
                else xns[:, 0:w * KD].rearrange("p (k n) -> p k n", k=KD) for n, w in PROJ_CHUNKS]

        size = dict(uq=3 * NQ, ukv=2 * D, wout=KD * D, proj=TILES * D_IN, vmla=TILES * MOBA, qT=HEADS * P,
                    mqT=HEADS // 2 * P, kT=HEADS * SEQ, mkT=HEADS // 2 * SEQ, pp=4 * SEQ, o=D, sums=2 * ATTN_HEADS)
        conv_size = dict(cin=KD * 2 * D, cout=KD * CHUNK, cb=CHUNK, uT=KD * (TAPS - 1 + SEQ), acc=D, v=D)
        arena = sb("arena", max(sum(size.values()), sum(conv_size.values())))
        at, part = 0, {}
        for k, n in size.items():
            part[k] = arena[:, at:at + n]
            at += n
        at = 0
        for k, n in conv_size.items():
            part[k] = arena[:, at:at + n]
            at += n
        uq = part["uq"].rearrange("p (k n) -> p k n", n=NQ)
        ukv = part["ukv"].rearrange("p (k n) -> p k n", n=D)
        wout = part["wout"].rearrange("p (k n) -> p k n", n=D)
        proj = [part["proj"][:, t * D_IN:(t + 1) * D_IN] for t in range(TILES)]
        vmla = [part["vmla"][:, t * MOBA:(t + 1) * MOBA] for t in range(TILES)]
        qT = part["qT"].rearrange("p (h t) -> p h t", h=HEADS)
        mqT = part["mqT"].rearrange("p (h t) -> p h t", h=HEADS // 2)
        kT = part["kT"].rearrange("p (h t) -> p h t", h=HEADS)
        mkT = part["mkT"].rearrange("p (h t) -> p h t", h=HEADS // 2)
        kfull = part["pp"][:, 0:NQ].rearrange("p (h d) -> p h d", h=HEADS)
        rtmp = [part[k][:, NQ:NQ + 256] for k in ("pp", "o")]
        pb = [part["pp"][:, i * SEQ:(i + 1) * SEQ] for i in range(2)]
        pT = [part["pp"][:, (2 + i) * SEQ:(3 + i) * SEQ].rearrange("p (k t) -> p k t", k=TILES) for i in range(2)]
        o = part["o"]
        qsb = o[:, 0:NQ]
        cT = hT_
        hT2_ = xns[:, 2 * D:3 * D].rearrange("p (k t) -> p k t", k=KD)
        hTs = [hT_, hT2_]
        cin = part["cin"].rearrange("p (j k n) -> p j k n", j=4, k=KD)
        kept = part["cin"][:, 0:(HEADS - KEPT_FROM) * HEAD_W]
        cout = part["cout"].rearrange("p (k n) -> p k n", k=KD)
        cbias = part["cb"]
        uT = part["uT"].rearrange("p (c t) -> p c t", c=KD)
        acc = part["acc"].rearrange("p (c t) -> p c t", c=KD)
        v = part["v"]
        sig = [v[:, i * P:(i + 1) * P] for i in range(2)]

        qq = sb("qq", 4 * P)
        q_t, q_T, eq = qq[:, 0:2 * P], qq[:, 2 * P:4 * P], qq
        sc = sb("sc", 2 * KEYS)
        sc2 = sb("sc2", 2 * KEYS)
        top = sb("top", 2 * TOPK)
        topi = sb("topi", 2 * TOPK, u32)
        topf = sb("topf", 2 * TOPK)
        best = sb("best", TOPK)
        pos = sb("pos", TOPK, u32)
        pos2 = sb("pos2", 2 * TOPK, u32)
        sel = sb("sel", 2 * TOPK)
        idx = [sb(f"idx{i}", RING, u32) for i in range(TOPK // RING)]
        nbest = sb("nbest", 1)
        e_g = sb("e_g", TOPK)
        e_sum = sb("e_sum", 1)
        e_inv = sb("e_inv", 1)
        g_next = sb("g_next", TOPK)
        g_cur = sb("g_cur", TOPK)
        dot = sb("dot", TOPK)
        gel = sb("gel", TOPK)
        coef = sb("coef", TOPK)
        diag = sb("diag", 2 * P)
        small = sb("small", 16)
        smalli = sb("smalli", 2, i32)
        posi = sb("posi", TILES, i32)
        posf = sb("posf", TILES)
        rows, rinv = part["sums"][:, 0:ATTN_HEADS], part["sums"][:, ATTN_HEADS:2 * ATTN_HEADS]
        nmax = small[:, 14:16]

        ypsum = ctx.enter_context(nc.psum_tensor("ypsum", [P, D], f32))
        qpsum = ctx.enter_context(nc.psum_tensor("qpsum", [P, CHUNK], f32))
        tpsum = ctx.enter_context(nc.psum_tensor("tpsum", [P, CHUNK], f32))
        spsum = ctx.enter_context(nc.psum_tensor("spsum", [P, CHUNK], f32))
        banks = [ctx.enter_context(nc.psum_tensor(f"bank{b}", [P, CHUNK], f32)) for b in range(BANKS)]
        banks += [qpsum, tpsum, spsum]

        consts_in = sem("consts_in")
        x_loaded = [sem(f"x_loaded{t}") for t in range(TILES)]
        win_in = [sem(f"win_in{n}") for n in range(len(PROJ_CHUNKS))]
        uq_in, ukv_in, wout_in = sem("uq_in"), sem("ukv_in"), sem("wout_in")
        head_in = sem("head_in")
        gain_in = [sem(f"gain_in{i}") for i in range(2)]
        cin_in = [sem(f"cin_in{j}") for j in range(4)]
        cout_in, cbias_in = sem("cout_in"), sem("cbias_in")
        out_sent = sem("out_sent")
        bank_full = [sem(f"bank_full{b}") for b in range(2 * BANKS)]
        bank_free = [sem(f"bank_free{b}") for b in range(2 * BANKS)]
        dve_step, act_step = sem("dve_step"), sem("act_step")
        hn_ready, xn_ready = sem("hn_ready"), sem("xn_ready")
        cn_ready, rope_ready, qpe_ready = sem("cn_ready"), sem("rope_ready"), sem("qpe_ready")
        max_ready, out_ready = sem("max_ready"), sem("out_ready")
        o_ready, x_mixed = sem("o_ready"), sem("x_mixed")
        sig_ready, acc_ready, z_ready, half_done = sem("sig_ready"), sem("acc_ready"), sem("z_ready"), sem("half_done")
        q_ready, q_copied, qT_ready, qT_copied = sem("q_ready"), sem("q_copied"), sem("qT_ready"), sem("qT_copied")
        s_ready, s_copied = sem("s_ready"), sem("s_copied")
        routed = [sem(f"routed{i}") for i in range(TOPK // RING)]
        best_ready, exp_ready, g_ready, g_taken = sem("best_ready"), sem("exp_ready"), sem("g_ready"), sem("g_taken")
        dot_ready, diag_ready, v_used = sem("dot_ready"), sem("diag_ready"), sem("v_used")
        ring_free, settled = sem("ring_free"), sem("settled")
        row_in = [sem(f"row_in{b}") for b in range(RING)]
        y_taken, final_ready, id_ready = sem("y_taken"), sem("final_ready"), sem("id_ready")

        def full(eng, j):
            eng.wait_ge(bank_full[bank_no(j)], turn_no(j) + 1)

        def emptied(eng, j):
            eng.wait_ge(bank_free[bank_no(j)], turn_no(j) + 1)

        def bank_of(eng, j):
            if turn_no(j):
                eng.wait_ge(bank_free[bank_no(j)], turn_no(j))
            return banks[bank_no(j)]

        def held(eng, signal, count):
            if not (isinstance(count, int) and count == 0):
                eng.wait_ge(signal, count)

        def settle(eng):
            eng.sem_inc(settled, 1)

        class Own:

            def __init__(self, eng, signal):
                self.eng, self.sem, self.n, self.turn = eng, signal, 0, 0

            def did(self, ins):
                ins.then_inc(self.sem, 1)
                self.n += 1

            def wait(self, back=0):
                self.eng.wait_ge(self.sem, self.turn + (self.n - back))

            def then(self, ins):
                self.did(ins)
                self.wait()

            @contextmanager
            def loop(self, i, times, per):
                start = self.n
                self.turn = i * per
                yield
                assert self.n - start == per, self.n - start
                self.turn, self.n = 0, start + per * times

        def out_half(t, i):
            return (t + i) % 2

        def load_conv_out(eng, n):
            if n:
                full(eng, CONV_AT[(n - 1) // 2] + J_CW + (n - 1) % 2)
            cs = out_half(n // 2, n % 2) * CHUNK
            eng.dma_start(part["cout"], c_out[:, cs * KD:(cs + CHUNK) * KD]).then_inc(cout_in, 16)

        def load_conv_bias(eng, n):
            if n:
                eng.wait_ge(half_done, n)
            cs = out_half(n // 2, n % 2) * CHUNK
            eng.dma_start(cbias, c_bout[0:1, cs:cs + CHUNK].to_broadcast([P, CHUNK])).then_inc(cbias_in, 16)

        block = ctx.enter_context(nc.Block())

        @block.sync
        def _(sp):
            sp.dma_start(xt(0), x_in[0:P, :]).then_inc(x_loaded[0], 16)
            for dst, src in ((ident[:, :], const_in[:, K_ID:K_ID + P]), (iota16[:, :], const_in[:, K_IOTA:K_IOTA + TOPK]),
                             (inv[:, :], const_in[:, K_INV:K_INV + NF]), (cols[:, :], cols_in[:, :]),
                             (eq[:, 0:SEQ], mask_in[:, :]), (posi[:, :], pos_in[:, :])):
                sp.dma_start(dst, src).then_inc(consts_in, 16)
            for c, (n, w) in enumerate(PROJ_CHUNKS):
                sp.dma_start(win_[c].rearrange("p k n -> p (k n)"), w_in[:, n * KD:(n + w) * KD]).then_inc(win_in[c], 16)
                if c == 0:
                    sp.dma_start(xt(1), x_in[P:SEQ, :]).then_inc(x_loaded[1], 16)
            sp.dma_start(part["uq"], w_uq[:, :]).then_inc(uq_in, 16)
            sp.dma_start(part["ukv"], w_ukv[:, :]).then_inc(ukv_in, 16)
            sp.dma_start(part["wout"], w_out[:, :]).then_inc(wout_in, 16)

            def load_gain(p):
                n = min(p // TILES, LAYERS)
                sp.dma_start(xn[p % 2], gains_in[n:n + 1, :].to_broadcast([P, D])).then_inc(gain_in[p % 2], 16)

            def load_head(layer, h):
                sp.dma_start(head[:, :], heads_in[layer][:, bass.ds(h * HEAD_W, HEAD_W)]).then_inc(head_in, 16)

            def keep_head(h):
                sp.dma_start(kept[:, bass.ds((h - KEPT_FROM) * HEAD_W, HEAD_W)], heads_in[1][:, bass.ds(h * HEAD_W, HEAD_W)])\
                  .then_inc(head_in, 16)

            load_head(0, 0)
            full(sp, PROJ_JOB[1][4])
            load_gain(0)
            for p in range(PHASES):
                sp.wait_ge(s_ready, p * HEADS + 1)
                load_head(p // TILES, 1)
                if p == 0:
                    full(sp, PROJ_JOB[1][3])
                else:
                    sp.wait_ge(y_taken, p)
                load_gain(p + 1)
                with sp.Fori(2, HEADS if p < 2 else KEPT_FROM) as h:
                    sp.wait_ge(s_ready, h + p * HEADS)
                    load_head(p // TILES, h)
                if p == 2:
                    full(sp, CONV_AT[1] + J_GLU + KD - 1)
                    with sp.Fori(KEPT_FROM, HEADS) as h:
                        sp.wait_ge(s_ready, h + p * HEADS)
                        keep_head(h)
                if p == 0:
                    sp.wait_ge(x_mixed, TILES)
                    for j in range(4):
                        n = KD * 2 * 256
                        sp.dma_start(part["cin"][:, j * n:(j + 1) * n], c_in[:, j * n:(j + 1) * n]).then_inc(cin_in[j], 16)
                    load_conv_out(sp, 0)
                    load_conv_bias(sp, 0)
                if p + 1 < PHASES:
                    sp.wait_ge(s_ready, (p + 1) * HEADS)
                    load_head((p + 1) // TILES, 0)
            for t in range(TILES):
                sp.wait_ge(final_ready, t + 1)
                sp.dma_start(out[t * P:(t + 1) * P, :], xt(t)).then_inc(out_sent, 16)
            sp.wait_ge(out_sent, 16 * TILES)

        @block.gpsimd
        def _(pool):
            pool.sem_inc(ring_free, RING)

            def gathers(p, h, last_chunks=False):
                for k in range(TOPK):
                    if k % RING == 0:
                        pool.wait_ge(routed[k // RING], h + (p * HEADS + 1))
                    if last_chunks and k in (4, 6):
                        full(pool, PROJ_JOB[1][WIN_AT.index(k // 2)])
                    b = k % RING
                    pool.wait_ge(ring_free, h * TOPK + (p * SLOTS + k + 1))
                    settle(pool)
                    pool.indirect_dma_start(
                        out=ring[:, b * 2 * D:(b + 1) * 2 * D], out_offset=None, in_=table[:, :],
                        in_offset=bass.IndirectOffsetOnAxis(ap=idx[k // RING][:, b:b + 1], axis=0)).then_inc(row_in[b], 16)

            full(pool, PROJ_JOB[1][2])
            gathers(0, 0, last_chunks=True)
            with pool.Fori(1, PHASES * HEADS) as h:
                gathers(0, h)

        @block.tensor
        def _(pe):
            def mm(o_, l, r, start, stop, **kw):
                return nc.tensor.matmul(o_, l, r, start=start, stop=stop, **kw)

            def transposes(j, srcs, rows_=P):
                bank = bank_of(pe, j)
                for i, s in enumerate(srcs):
                    last = nc.tensor.transpose(bank[0:rows_, i * P:(i + 1) * P], s, ident[:, :])
                last.then_inc(bank_full[bank_no(j)], 1)

            def turn_over(j, src):
                for i in range(2):
                    transposes(j + i, [src[:, (4 * i + k) * P:(4 * i + k + 1) * P] for k in range(4)])

            def gemm(j, lhs, rhs, width, half=None):
                bank = banks[bank_no(j)] if half == 1 else bank_of(pe, j)
                n = len(lhs)
                for k in range(n // 2 if half == 1 else 0, n // 2 if half == 0 else n):
                    last = mm(bank[:, 0:width], lhs[k], rhs[k], k == 0, k == n - 1)
                if half != 0:
                    last.then_inc(bank_full[bank_no(j)], 1)

            def turn_normed(t):
                pe.wait_ge(hn_ready, t + 1)
                turn_over(PROJ_AT[t], o)

            def project(t, c, ks=range(KD)):
                n, w = PROJ_CHUNKS[c]
                j = PROJ_JOB[t][c]
                if c == 0:
                    emptied(pe, PROJ_AT[t])
                    emptied(pe, PROJ_AT[t] + 1)
                if t == 0:
                    pe.wait_ge(win_in[c], 16)
                bank = bank_of(pe, j) if ks[0] == 0 else banks[bank_no(j)]
                for k in ks:
                    last = mm(bank[:, 0:w], hTs[t][:, k, :], win_[c][:, k, :], k == 0, k == KD - 1)
                if ks[-1] == KD - 1:
                    last.then_inc(bank_full[bank_no(j)], 1)

            def turn_output(k):
                emptied(pe, MIX_AT[0] + J_HEAD + 3 * (2 * k) + 2)
                emptied(pe, MIX_AT[0] + J_HEAD + 3 * (2 * k + 1) + 2)
                transposes(OUT_AT + k, [o[:, k * P:(k + 1) * P]])

            def add_output(k):
                emptied(pe, OUT_AT + k)
                if k == 0:
                    pe.wait_ge(wout_in, 16)
                for half in range(2):
                    last = mm(ypsum[:, half * CHUNK:(half + 1) * CHUNK], hT_[:, k, :], wout[:, k, half * CHUNK:(half + 1) * CHUNK],
                              k == 0, k == KD - 1)
                if k == KD - 1:
                    last.then_inc(out_ready, 1)

            def fill(a):
                if a < 2:
                    project(1, 4, range(4 * a, 4 * a + 4))
                if a - 1 in OUT_HEADS:
                    add_output(OUT_HEADS.index(a - 1))
                if a in OUT_HEADS:
                    turn_output(OUT_HEADS.index(a))

            def latents(t):
                J = MIX_AT[t]
                pe.wait_ge(cn_ready, t + 1)
                transposes(J + J_C, [proj[t][:, i * P:(i + 1) * P] for i in range(3)])
                transposes(J + J_C + 1, [proj[t][:, OFF_KV + i * P:OFF_KV + (i + 1) * P] for i in range(2)])

            def queries(t, i):
                w = (CHUNK, NQ - CHUNK)[i]
                if i == 0:
                    emptied(pe, MIX_AT[t] + J_C)
                    pe.wait_ge(uq_in, 16)
                gemm(MIX_AT[t] + J_U + i, [cT[:, k, :] for k in range(3)], [uq[:, k, i * CHUNK:i * CHUNK + w] for k in range(3)], w)

            def keys_values(t, i):
                if i == 0:
                    emptied(pe, MIX_AT[t] + J_C + 1)
                    pe.wait_ge(ukv_in, 16)
                gemm(MIX_AT[t] + J_KV + i, [cT[:, 3 + k, :] for k in range(2)],
                     [ukv[:, k, i * CHUNK:(i + 1) * CHUNK] for k in range(2)], CHUNK)

            def turn_queries(t):
                pe.wait_ge(qpe_ready, t + 1)
                for i in range(2):
                    transposes(MIX_AT[t] + J_QT + i, [qsb[:, (4 * i + h) * QK:(4 * i + h + 1) * QK] for h in range(4)], QK)

            def turn_keys(t):
                emptied(pe, MIX_AT[t] + J_KV)
                pe.wait_ge(rope_ready, t + 1)
                for i in range(2):
                    transposes(MIX_AT[t] + J_KT + i, [kfull[:, 4 * i + h, :] for h in range(4)], QK)

            def turn_moba(t):
                for j, off in ((J_MQT, OFF_MQ), (J_MKT, OFF_MK)):
                    transposes(MIX_AT[t] + j, [proj[t][:, off + i * P:off + (i + 1) * P] for i in range(4)])

            def scores(t, a):
                j, W = MIX_AT[t] + J_HEAD + 3 * a, (t + 1) * P
                if a == 0:
                    for i in range(MIX_AT[t] + J_QT, MIX_AT[t] + J_HEAD):
                        emptied(pe, i)
                bank = bank_of(pe, j)
                mm(bank[:, 0:W], ident16[:, :], mask16[:, SEQ - W:SEQ], True, False)
                if a < HEADS:
                    l, r = qT[0:QK, a, :], kT[0:QK, a, 0:W]
                else:
                    b, s = (a - HEADS) // 2, HD * (a % 2)
                    l, r = mqT[s:s + HD, b, :], mkT[s:s + HD, b, 0:W]
                mm(bank[:, 0:W], l, r, False, True).then_inc(bank_full[bank_no(j)], 1)

            def turn_weights(t, a):
                j = MIX_AT[t] + J_HEAD + 3 * a
                emptied(pe, j)
                transposes(j + 1, [pb[a % 2][:, s * P:(s + 1) * P] for s in range(t + 1)])

            def weigh_values(t, a):
                j = MIX_AT[t] + J_HEAD + 3 * a
                emptied(pe, j + 1)
                vals = [vmla[s][:, a * VD:(a + 1) * VD] if a < HEADS else
                        proj[s][:, OFF_MV + (a - HEADS) * HD:OFF_MV + (a - HEADS + 1) * HD] for s in range(t + 1)]
                gemm(j + 2, [pT[a % 2][:, s, :] for s in range(t + 1)], vals, VD)

            def turn_outputs(t):
                pe.wait_ge(o_ready, 1)
                turn_over(MIX_AT[t] + J_OT, o)

            def mix_out(t, i, half=None):
                if i == 0 and half != 1:
                    emptied(pe, MIX_AT[t] + J_OT)
                    emptied(pe, MIX_AT[t] + J_OT + 1)
                    pe.wait_ge(wout_in, 16)
                gemm(MIX_AT[t] + J_W + i, [hT_[:, k, :] for k in range(KD)],
                     [wout[:, k, i * CHUNK:(i + 1) * CHUNK] for k in range(KD)], CHUNK, half)

            def glu(t, c):
                j = CONV_AT[t] + J_GLU + c
                if c == 0:
                    emptied(pe, CONV_AT[t])
                    emptied(pe, CONV_AT[t] + 1)
                if t == 0 and c % 2 == 0:
                    pe.wait_ge(cin_in[c // 2], 16)
                bank = bank_of(pe, j)
                for g in range(2):
                    cs = g * 256 + (c % 2) * P
                    for k in range(KD):
                        last = mm(bank[:, g * P:(g + 1) * P], cin[:, c // 2, k, cs:cs + P], hT_[:, k, :], k == 0, k == KD - 1)
                last.then_inc(bank_full[bank_no(j)], 1)

            def conv_out(t, i, half):
                if half == 0:
                    if i == 0:
                        emptied(pe, CONV_AT[t] + J_Z)
                        emptied(pe, CONV_AT[t] + J_Z + 1)
                    pe.wait_ge(cout_in, 16 * (t + i + 1))
                gemm(CONV_AT[t] + J_CW + i, [hT_[:, k, :] for k in range(KD)], [cout[:, k, :] for k in range(KD)], CHUNK, half)

            def beside_attention(s):
                if s == 4:
                    latents(1)
                if s in (6, 7):
                    queries(1, s - 6)
                if s in (9, 10):
                    keys_values(1, s - 9)
                if s == 15:
                    turn_queries(1)
                if s == 19:
                    turn_keys(1)
                if s == 21:
                    turn_moba(1)
                if s == 23:
                    scores(1, 0)
                a, r = divmod(s - HEAD_SLOT, 3)
                if 0 <= a < ATTN_HEADS and r == 0:
                    turn_weights(1, a)
                    if a + 1 < ATTN_HEADS:
                        scores(1, a + 1)
                if 0 <= a < ATTN_HEADS and r == 2:
                    weigh_values(1, a)
                if s == 75:
                    turn_outputs(1)
                if s in (77, 78, 79, 80):
                    mix_out(1, (s - 77) // 2, (s - 77) % 2)
                beside_norm(0, s)

            def beside_conv(p, s):
                t = p - 1
                if s == 4:
                    pe.wait_ge(hn_ready, TILES + t + 1)
                    turn_over(CONV_AT[t], v)
                if s in GLU_SLOTS:
                    glu(t, GLU_SLOTS.index(s))
                if s == 84:
                    pe.wait_ge(acc_ready, t + 1)
                    turn_over(CONV_AT[t] + J_ACC, part["acc"])
                if s == 92:
                    pe.wait_ge(z_ready, t + 1)
                    turn_over(CONV_AT[t] + J_Z, v)
                if s in (94, 95):
                    conv_out(t, 0, s - 94)
                if s in (105, 106):
                    conv_out(t, 1, s - 105)
                beside_norm(p, s)

            def beside_norm(p, s):
                if s == 110:
                    pe.wait_ge(xn_ready, p + 2)
                    turn_over(NORM_AT[p + 1], xn[(p + 1) % 2])

            def peer_q(H, first=None, at_=None, load=True):
                if first is not None:
                    emptied(pe, NORM_AT[first])
                    emptied(pe, NORM_AT[first] + 1)
                if load:
                    pe.wait_ge(head_in, (H + 1) * 16)
                held(pe, q_copied, H)
                for k in range(KD):
                    last = mm(qpsum[:, 0:2 * HALF], xnT[:, k, :],
                              wq_[:, k, :] if at_ is None else kept[:, bass.ds(at_ + k * 2 * HALF, 2 * HALF)], k == 0, k == KD - 1)
                last.then_inc(q_ready, 1)

            def peer_qT(H):
                pe.wait_ge(q_copied, H + 1)
                held(pe, qT_copied, H)
                for c in range(2):
                    last = nc.tensor.transpose(tpsum[:, c * P:(c + 1) * P], q_t[:, c * HALF:(c + 1) * HALF], ident[:, :])
                last.then_inc(qT_ready, 1)

            def peer_scores(H, at_=None):
                pe.wait_ge(qT_copied, H + 1)
                held(pe, s_copied, H)
                for c in range(2):
                    last = mm(spsum[:, c * KEYS:(c + 1) * KEYS], q_T[:, c * P:(c + 1) * P],
                              skT[:, c * KEYS:(c + 1) * KEYS] if at_ is None else
                              kept[:, bass.ds(at_ + (KD * 2 * HALF + c * KEYS), KEYS)], True, True)
                last.then_inc(s_ready, 1)

            def peer_slot(H, k, stop=False):
                pe.wait_ge(diag_ready, H * TOPK + (k + 1))
                b = k % RING
                for half in range(2):
                    last = mm(ypsum[:, half * CHUNK:(half + 1) * CHUNK], diag[:, (k % 2) * P:(k % 2 + 1) * P],
                              ring[:, b * 2 * D + D + half * CHUNK:b * 2 * D + D + (half + 1) * CHUNK], False, stop,
                              skip_group_check=True)
                last.then_inc(ring_free, 1)

            def peer_seed(p):
                if p:
                    pe.wait_ge(y_taken, p)
                for half in range(2):
                    mm(ypsum[:, half * CHUNK:(half + 1) * CHUNK], ident[:, :],
                       xt(p % TILES)[:, half * CHUNK:(half + 1) * CHUNK], True, False, skip_group_check=True)

            def peer_head(H, N, stop=False, first=None, beside=None, s=0, at_=None, load=True):
                for k in range(TOPK):
                    peer_slot(H, k, stop=stop and k == TOPK - 1)
                    if N is not None and k == 0:
                        peer_q(N, first, at_, load)
                    if N is not None and k == 1:
                        peer_qT(N)
                    if N is not None and k == 2:
                        peer_scores(N, at_)
                    if beside is not None:
                        beside(s + k)

            def heads(p, h0, h1, kept_=False):
                with pe.Fori(h0, h1) as h:
                    at_ = (h - (KEPT_FROM - 1)) * HEAD_W if kept_ else None
                    peer_head(h + p * HEADS, h + (p * HEADS + 1), at_=at_, load=not kept_ or p == 2)

            def busy_heads(p, h0, h1, beside):
                for h in range(h0, h1):
                    at_ = (h + 1 - KEPT_FROM) * HEAD_W if p == 2 and h + 1 >= KEPT_FROM else None
                    peer_head(h + p * HEADS, h + p * HEADS + 1, beside=beside, s=h * TOPK, at_=at_)

            def last_head(p):
                N = (p + 1) * HEADS
                if p + 1 < PHASES:
                    peer_head(N - 1, N, stop=True, first=p + 1)
                    peer_seed(p + 1)
                else:
                    peer_head(N - 1, None, stop=True)

            pe.wait_ge(consts_in, 6 * 16)
            for t in range(TILES):
                turn_normed(t)
            for c in range(len(PROJ_CHUNKS)):
                project(0, c)
            project(1, 0)
            latents(0)
            for i in range(2):
                queries(0, i)
            for i in range(2):
                keys_values(0, i)
            turn_queries(0)
            turn_keys(0)
            turn_moba(0)
            pe.wait_ge(id_ready, 1)
            scores(0, 0)
            for a in range(ATTN_HEADS):
                turn_weights(0, a)
                if a + 1 < ATTN_HEADS:
                    scores(0, a + 1)
                fill(a)
                weigh_values(0, a)
            turn_output(KD - 1)
            add_output(KD - 1)
            project(1, 2)
            pe.wait_ge(xn_ready, 1)
            turn_over(NORM_AT[0], xn[0])
            peer_seed(0)
            for k in range(KD - BANKS + 1, KD + 1):
                emptied(pe, OUT_AT + k)
            peer_q(0, first=0)
            peer_qT(0)
            peer_scores(0)
            project(1, 1)
            project(1, 3)
            busy_heads(0, 0, 7, beside_attention)
            last_head(0)
            for p in (1, 2):
                busy_heads(p, 0, 3, lambda s: beside_conv(p, s))
                heads(p, KEPT_FROM - 1, 5, kept_=p == 2)
                busy_heads(p, 5, 7, lambda s: beside_conv(p, s))
                last_head(p)
            heads(3, 0, KEPT_FROM - 1)
            heads(3, KEPT_FROM - 1, 7, kept_=True)
            last_head(3)

        @block.scalar
        def _(act):
            own = Own(act, act_step)

            def run(out_, in_, func=ACT.Copy, **kw):
                return nc.scalar.activation(out_, in_, func, **kw)

            def free(j, ins):
                ins.then_inc(bank_free[bank_no(j)], 1)

            def take(j, out_, n=CHUNK, rows_=P, **kw):
                full(act, j)
                free(j, run(out_, banks[bank_no(j)][0:rows_, 0:n], **kw))

            def take_scaled(j, dst, k0, count, col):
                full(act, j)
                for i in range(count):
                    last = run(dst[:, k0 + i, :], banks[bank_no(j)][:, i * P:(i + 1) * P], scale=cols[:, col + i:col + i + 1])
                free(j, last)

            def turn_normed(t):
                for i in range(2):
                    take_scaled(PROJ_AT[t] + i, hTs[t], 4 * i, 4, C_MIX + 4 * i)

            def project(t, c):
                n, w = PROJ_CHUNKS[c]
                take(PROJ_JOB[t][c], proj[t][:, n:n + w], w)

            def output_block(k):
                take(OUT_AT + k, hT_[:, k, :], P)

            def latents(t):
                J = MIX_AT[t]
                if t:
                    act.wait_ge(x_mixed, t)
                take_scaled(J + J_C, cT, 0, 3, C_QN)
                take_scaled(J + J_C + 1, cT, 3, 2, C_KVN)

            def queries(t, i):
                w = (CHUNK, NQ - CHUNK)[i]
                take(MIX_AT[t] + J_U + i, qsb[:, i * CHUNK:i * CHUNK + w], w)

            def keys_values(t, i):
                j = MIX_AT[t] + J_KV + i
                if i == 0:
                    full(act, j)
                    free(j, run(kfull[:, :, 0:NOPE], banks[bank_no(j)][:, :].rearrange("p (h d) -> p h d", h=HEADS)))
                else:
                    take(j, vmla[t])

            def turned_keys(j, dst, rows_):
                full(act, j)
                free(j, run(dst, banks[bank_no(j)][0:rows_, :].rearrange("p (h t) -> p h t", h=4)))

            def turn_queries(t):
                for i in range(2):
                    take(MIX_AT[t] + J_QT + i, qT[0:QK, 4 * i:4 * i + 4, :].rearrange("p h t -> p (h t)"), rows_=QK, scale=QK ** -0.5)

            def turn_keys(t):
                for i in range(2):
                    turned_keys(MIX_AT[t] + J_KT + i, kT[0:QK, 4 * i:4 * i + 4, t * P:(t + 1) * P], QK)

            def turn_moba(t):
                take(MIX_AT[t] + J_MQT, mqT[:, :, :].rearrange("p h t -> p (h t)"), scale=HD ** -0.5)
                turned_keys(MIX_AT[t] + J_MKT, mkT[:, :, t * P:(t + 1) * P], P)

            def exponentials(t, a):
                j, W = MIX_AT[t] + J_HEAD + 3 * a, (t + 1) * P
                act.wait_ge(max_ready, t * ATTN_HEADS + a + 1)
                if a >= 2:
                    emptied(act, j - 5)
                free(j, run(pb[a % 2][:, 0:W], banks[bank_no(j)][:, 0:W], ACT.Exp,
                            bias=nmax[:, a % 2:a % 2 + 1], accum_out=rows[:, a:a + 1]))

            def turn_outputs(t):
                for i in range(2):
                    take(MIX_AT[t] + J_OT + i, hT[:, i * CHUNK:(i + 1) * CHUNK])

            def glu(t, c):
                j = CONV_AT[t] + J_GLU + c
                full(act, j)
                if c >= 2:
                    emptied(act, j - 2)
                run(sig[c % 2], banks[bank_no(j)][:, P:2 * P], ACT.Sigmoid,
                    bias=cols[:, C_BIN + KD + c:C_BIN + KD + c + 1]).then_inc(sig_ready, 1)

            def silu(t, i):
                j = CONV_AT[t] + J_Z + i
                full(act, j)
                for k in range(4):
                    c = 4 * i + k
                    last = run(hT_[:, c, :], banks[bank_no(j)][:, k * P:(k + 1) * P], ACT.Silu,
                               scale=cols[:, C_LNG + c:C_LNG + c + 1], bias=cols[:, C_LNB + c:C_LNB + c + 1])
                free(j, last)

            def beside_attention(s):
                if s == 5:
                    latents(1)
                if s in (7, 8):
                    queries(1, s - 7)
                if s in (10, 11):
                    keys_values(1, s - 10)
                if s == 16:
                    turn_queries(1)
                if s == 20:
                    turn_keys(1)
                if s == 22:
                    turn_moba(1)
                if s == HEAD_SLOT - 1:
                    exponentials(1, 0)
                a, r = divmod(s - HEAD_SLOT, 3)
                if 0 <= a < ATTN_HEADS - 1 and r == 2:
                    exponentials(1, a + 1)
                if s == 76:
                    turn_outputs(1)
                beside_norm(0, s)

            def beside_conv(p, s):
                t = p - 1
                J = CONV_AT[t]
                if s == 5:
                    if t:
                        act.wait_ge(half_done, 2 * t)
                    for i in range(2):
                        take_scaled(J + i, hT_, 4 * i, 4, C_MIX + KD + 4 * i)
                if s - 1 in GLU_SLOTS:
                    glu(t, GLU_SLOTS.index(s - 1))
                if s == 85:
                    for i in range(2):
                        take(J + J_ACC + i, v[:, i * CHUNK:(i + 1) * CHUNK])
                if s == 93:
                    for i in range(2):
                        silu(t, i)
                if s == 96:
                    load_conv_out(act, 2 * t + 1)
                if s == 98:
                    load_conv_bias(act, 2 * t + 1)
                beside_norm(p, s)

            def beside_norm(p, s):
                if s == 111:
                    for i in range(2):
                        take(NORM_AT[p + 1] + i, xnT_[:, i * CHUNK:(i + 1) * CHUNK])

            def peer_copy(H, ready, copied, dst, psum, used):
                act.wait_ge(ready, H + 1)
                held(act, used, H)
                if dst is q_t:
                    held(act, routed[0], H)
                run(dst[:, :], psum[:, 0:2 * P]).then_inc(copied, 1)

            def peer_exp(H):
                act.wait_ge(best_ready, H + 1)
                run(e_g[:, :], best[:, :], ACT.Exp, bias=nbest[:, 0:1], accum_out=e_sum[:, 0:1]).then_inc(exp_ready, 1)

            def peer_gates(H):
                act.wait_ge(g_ready, H + 1)
                run(g_cur[:, :], g_next[:, :]).then_inc(g_taken, 1)
                act.wait_ge(g_taken, H + 1)

            def peer_slot(H, k, first=False):
                act.wait_ge(dot_ready, H * TOPK + (k + 1))
                own.then(run(gel[:, k:k + 1], dot[:, k:k + 1], ACT.Gelu))
                own.then(run(coef[:, k:k + 1], gel[:, k:k + 1], scale=g_cur[:, k:k + 1]))
                if not (first and k < 2):
                    act.wait_ge(ring_free, H * TOPK + (k - 1 + RING))
                run(diag[:, (k % 2) * P:(k % 2 + 1) * P], ident[:, :], scale=coef[:, k:k + 1]).then_inc(diag_ready, 1)

            def peer_head(H, N, beside=None, s=0):
                peer_gates(H)
                for k in range(TOPK):
                    peer_slot(H, k)
                    if N is not None and k == 1:
                        peer_copy(N, q_ready, q_copied, q_t, qpsum, qT_ready)
                    if N is not None and k == 2:
                        peer_copy(N, qT_ready, qT_copied, q_T, tpsum, s_ready)
                    if N is not None and k == 3:
                        peer_copy(N, s_ready, s_copied, sc, spsum, routed[0])
                    if N is not None and k == 8:
                        peer_exp(N)
                    if beside is not None:
                        beside(s + k)

            def heads(p, h0, h1):
                with act.Fori(h0, h1) as h:
                    with own.loop(h - h0, h1 - h0, 2 * TOPK):
                        peer_head(h + p * HEADS, h + (p * HEADS + 1))

            def busy_heads(p, h0, h1, beside):
                for h in range(h0, h1):
                    peer_head(h + p * HEADS, h + p * HEADS + 1, beside, h * TOPK)

            def last_head(p):
                N = (p + 1) * HEADS
                peer_head(N - 1, N if p + 1 < PHASES else None)

            act.wait_ge(consts_in, 6 * 16)
            for t in range(TILES):
                turn_normed(t)
            project(0, 0)
            project(0, 1)
            act.wait_ge(id_ready, 2)
            run(trig[:, :], trig[:, :], ACT.Sin).then_inc(id_ready, 1)
            for c in range(2, len(PROJ_CHUNKS)):
                project(0, c)
            project(1, 0)
            latents(0)
            for i in range(2):
                queries(0, i)
            for i in range(2):
                keys_values(0, i)
            turn_queries(0)
            turn_keys(0)
            turn_moba(0)
            for a in range(ATTN_HEADS):
                exponentials(0, a)
                if a == 2:
                    project(1, 4)
                if a - 1 in OUT_HEADS:
                    output_block(OUT_HEADS.index(a - 1))
            output_block(KD - 1)
            project(1, 2)
            for i in range(2):
                take(NORM_AT[0] + i, xnT_[:, i * CHUNK:(i + 1) * CHUNK])
            peer_copy(0, q_ready, q_copied, q_t, qpsum, qT_ready)
            peer_copy(0, qT_ready, qT_copied, q_T, tpsum, s_ready)
            peer_copy(0, s_ready, s_copied, sc, spsum, routed[0])
            project(1, 1)
            peer_exp(0)
            project(1, 3)
            busy_heads(0, 0, 7, beside_attention)
            last_head(0)
            for p in (1, 2):
                busy_heads(p, 0, 3, lambda s: beside_conv(p, s))
                heads(p, 3, 5)
                busy_heads(p, 5, 7, lambda s: beside_conv(p, s))
                last_head(p)
            heads(3, 0, 7)
            last_head(3)

        @block.vector
        def _(dve):
            own = Own(dve, dve_step)
            V = nc.vector

            def free(j, ins):
                ins.then_inc(bank_free[bank_no(j)], 1)

            def power(var, w, y, tmp):
                yi, vi = y.bitcast(i32), var.bitcast(i32)
                own.then(V.tensor_scalar(smalli[:, 0:w], vi, 1, None, ALU.logical_shift_right))
                own.then(V.tensor_scalar(yi, smalli[:, 0:w], -1.0, float(0x5f3759df), ALU.mult, ALU.add))
                for _ in range(3):
                    own.then(V.scalar_tensor_tensor(out=tmp, in0=y, scalar=-0.5, in1=y, op0=ALU.mult, op1=ALU.mult))
                    own.then(V.tensor_tensor(tmp, tmp, var, ALU.mult))
                    own.then(V.scalar_tensor_tensor(out=y, in0=tmp, scalar=1.5, in1=y, op0=ALU.add, op1=ALU.mult))

            def mean_square(src, n, c):
                own.then(V.tensor_tensor_reduce(out=junk[:, 0:n], in0=src, in1=src, scale=1.0, scalar=0.0,
                                                op0=ALU.mult, op1=ALU.add, accum_out=small[:, c:c + 1]))
                own.then(V.tensor_scalar(small[:, c:c + 1], small[:, c:c + 1], 1.0 / n, EPS, ALU.mult, ALU.add))

            def rms(src, n):
                mean_square(src, n, 0)
                power(small[:, 0:1], 1, small[:, 2:3], small[:, 4:5])
                return small[:, 2:3]

            def project(t):
                dve.wait_ge(x_loaded[t], 16)
                r = rms(xt(t), D)
                if t:
                    emptied(dve, PROJ_AT[t - 1] + 1)
                V.tensor_scalar(o, xt(t), r, None, ALU.mult).then_inc(hn_ready, 1)

            def rotate(src, heads, half, t, f0):
                c = trig[:, t * 2 * NF + f0:t * 2 * NF + f0 + half].unsqueeze(1).to_broadcast([P, heads, half])
                s = trig[:, t * 2 * NF + NF + f0:t * 2 * NF + NF + f0 + half].unsqueeze(1).to_broadcast([P, heads, half])
                x1, x2 = src[:, :, 0:half], src[:, :, half:2 * half]
                a, b = (r[:, 0:heads * half].rearrange("p (h d) -> p h d", h=heads) for r in rtmp)
                own.did(V.tensor_tensor(a, x1, s, ALU.mult))
                own.then(V.tensor_tensor(b, x2, s, ALU.mult))
                own.did(V.tensor_tensor(x1, x1, c, ALU.mult))
                own.then(V.tensor_tensor(x2, x2, c, ALU.mult))
                own.did(V.tensor_tensor(x1, x1, b, ALU.subtract))
                own.then(V.tensor_tensor(x2, x2, a, ALU.add))

            def latents(t):
                for c in range(len(PROJ_CHUNKS)):
                    emptied(dve, PROJ_JOB[t][c])
                mean_square(proj[t][:, 0:Q_LORA], Q_LORA, 0)
                mean_square(proj[t][:, OFF_KV:OFF_ROPE], KV_LORA, 1)
                power(small[:, 0:2], 2, small[:, 2:4], small[:, 4:6])
                V.tensor_scalar(proj[t][:, 0:Q_LORA], proj[t][:, 0:Q_LORA], small[:, 2:3], None, ALU.mult)
                V.tensor_scalar(proj[t][:, OFF_KV:OFF_ROPE], proj[t][:, OFF_KV:OFF_ROPE], small[:, 3:4], None, ALU.mult)\
                 .then_inc(cn_ready, 1)

            def rotate_key(t):
                dve.wait_ge(id_ready, 3)
                if t == 0:
                    emptied(dve, PROJ_AT[1] + 1)
                rotate(proj[t][:, OFF_ROPE:OFF_MQ].unsqueeze(1), 1, ROPE // 2, t, 0)
                own.did(V.tensor_copy(kfull[:, :, NOPE:QK], proj[t][:, OFF_ROPE:OFF_MQ].unsqueeze(1).to_broadcast([P, HEADS, ROPE])))

            def rotate_moba(t, off):
                rotate(proj[t][:, off:off + MOBA].rearrange("p (h d) -> p h d", h=HEADS), HEADS, HD // 2, t, ROPE // 2)
                if off == OFF_MK:
                    dve.sem_inc(rope_ready, 1)

            def rotate_queries(t):
                for i in range(2):
                    emptied(dve, MIX_AT[t] + J_U + i)
                rotate(qsb.rearrange("p (h d) -> p h d", h=HEADS)[:, :, NOPE:QK], HEADS, ROPE // 2, t, 0)
                dve.sem_inc(qpe_ready, 1)

            def maximum(t, a):
                j = MIX_AT[t] + J_HEAD + 3 * a
                full(dve, j)
                V.tensor_reduce(nmax[:, a % 2:a % 2 + 1], banks[bank_no(j)][:, 0:(t + 1) * P], AX.X, ALU.max, negate=True)\
                 .then_inc(max_ready, 1)

            def turn_weights(t, a):
                j = MIX_AT[t] + J_HEAD + 3 * a + 1
                full(dve, j)
                if a == 0:
                    emptied(dve, MIX_AT[t] + J_KT + 1)
                free(j, V.tensor_copy(pT[a % 2][:, 0:t + 1, :].rearrange("p s t -> p (s t)"), banks[bank_no(j)][:, 0:(t + 1) * P]))

            def normalise(t, a):
                j = MIX_AT[t] + J_HEAD + 3 * a + 2
                own.then(V.reciprocal(rinv[:, a:a + 1], rows[:, a:a + 1]))
                full(dve, j)
                free(j, V.tensor_scalar(o[:, a * VD:(a + 1) * VD], banks[bank_no(j)][:, 0:VD], rinv[:, a:a + 1], None, ALU.mult))
                if t and a == ATTN_HEADS - 1:
                    emptied(dve, j)
                    dve.sem_inc(o_ready, 1)

            def mix_out(t, i):
                j = MIX_AT[t] + J_W + i
                full(dve, j)
                xs = xt(t)[:, i * CHUNK:(i + 1) * CHUNK]
                free(j, V.tensor_tensor(xs, xs, banks[bank_no(j)][:, :], ALU.add))
                if i == 1:
                    emptied(dve, j - 1)
                    emptied(dve, j)
                    dve.sem_inc(x_mixed, 1)

            def conv_norm_in(t):
                r = rms(xt(t), D)
                V.tensor_scalar(v, xt(t), r, None, ALU.mult).then_inc(hn_ready, 1)
                if t == 0:
                    own.did(V.memset(uT[:, :, 0:TAPS - 1], 0.0))

            def glu(t, c):
                j = CONV_AT[t] + J_GLU + c
                dve.wait_ge(sig_ready, t * KD + c + 1)
                full(dve, j)
                free(j, V.scalar_tensor_tensor(out=uT[:, c, TAPS - 1 + t * P:TAPS - 1 + (t + 1) * P],
                                               in0=banks[bank_no(j)][:, 0:P], scalar=cols[:, C_BIN + c:C_BIN + c + 1],
                                               in1=sig[c % 2], op0=ALU.add, op1=ALU.mult))

            def first_tap(t, g):
                cs = range(g * KD // 2, (g + 1) * KD // 2)
                for c in cs:
                    emptied(dve, CONV_AT[t] + J_GLU + c)
                for c in cs:
                    own.did(V.tensor_scalar(acc[:, c, :], uT[:, c, t * P:(t + 1) * P], cols[:, C_TAPS + c * TAPS:C_TAPS + c * TAPS + 1],
                                            cols[:, C_BDW + c:C_BDW + c + 1], ALU.mult, ALU.add))

            def tap(t, g, k):
                for c in range(g * KD // 2, (g + 1) * KD // 2):
                    own.wait(KD // 2 - 1)
                    own.did(V.scalar_tensor_tensor(
                        out=acc[:, c, :], in0=uT[:, c, bass.ds(k + t * P, P)],
                        scalar=cols[:, bass.ds(k + (C_TAPS + c * TAPS), 1)], in1=acc[:, c, :], op0=ALU.mult, op1=ALU.add))

            def taps_done():
                own.wait()
                dve.sem_inc(acc_ready, 1)

            def conv_norm(t):
                J = CONV_AT[t]
                for i in range(2):
                    emptied(dve, J + J_ACC + i)
                    own.did(V.bn_stats(small[:, 0:6] if i == 0 else eqs, v[:, i * CHUNK:(i + 1) * CHUNK]))
                own.wait()
                own.then(V.bn_aggr(small[:, 12:14], small[:, 0:12]))
                own.then(V.tensor_scalar(small[:, 0:1], small[:, 13:14], EPS, None, ALU.add))
                power(small[:, 0:1], 1, small[:, 2:3], small[:, 4:5])
                V.tensor_scalar(v, v, small[:, 12:13], small[:, 2:3], ALU.subtract, ALU.mult).then_inc(z_ready, 1)

            eqs = small[:, 6:12]

            def conv_out(t, i):
                j = CONV_AT[t] + J_CW + i
                full(dve, j)
                n = out_half(t, i) * CHUNK
                xs = xt(t)[:, n:n + CHUNK]
                free(j, V.tensor_tensor(xs, xs, banks[bank_no(j)][:, :], ALU.add))
                emptied(dve, j)
                dve.wait_ge(cbias_in, 16 * (t + i + 1))
                V.tensor_tensor(xs, xs, cbias, ALU.add).then_inc(half_done, 1)
                dve.wait_ge(half_done, 2 * t + i + 1)

            def route(H, layer, part_):
                top_, topi_, topf_ = (r[:, :].rearrange("p (c k) -> p c k", c=2) for r in (top, topi, topf))
                sc_, sc2_ = (r[:, :].rearrange("p (c k) -> p c k", c=2) for r in (sc, sc2))
                low = -3.0e38
                if part_ == 0:
                    dve.wait_ge(s_copied, H + 1)
                    settle(dve)
                    for c in range(2):
                        own.did(V.max(top_[:, c, 0:8], sc_[:, c, :]))
                    for c in range(2):
                        own.wait(1)
                        settle(dve)
                        own.did(V.max_index(topi_[:, c, 0:8], top_[:, c, 0:8], sc_[:, c, :]))
                        own.did(V.match_replace(sc2_[:, c, :], top_[:, c, 0:8], sc_[:, c, :], low))
                    own.wait()
                if part_ == 1:
                    settle(dve)
                    for c in range(2):
                        own.did(V.max(top_[:, c, 8:16], sc2_[:, c, :]))
                    for c in range(2):
                        own.wait(1)
                        settle(dve)
                        own.did(V.max_index(topi_[:, c, 8:16], top_[:, c, 8:16], sc2_[:, c, :]))
                    own.wait()
                    own.did(V.tensor_scalar(topf_[:, 0, :], topi_[:, 0, :], float(layer * KEYS), None, ALU.add))
                    own.did(V.tensor_copy(topf_[:, 1, :], topi_[:, 1, :]))
                cand, cand2 = sc2, sc
                if part_ == 2:
                    own.then(V.tensor_tensor(cand[:, :].rearrange("p (a b) -> p a b", a=TOPK),
                                             top_[:, 0, :].unsqueeze(2).to_broadcast([P, TOPK, TOPK]),
                                             top_[:, 1, :].unsqueeze(1).to_broadcast([P, TOPK, TOPK]), ALU.add))
                    settle(dve)
                    own.then(V.max(best[:, 0:8], cand[:, :]))
                    settle(dve)
                    own.did(V.max_index(pos[:, 0:8], best[:, 0:8], cand[:, :]))
                    own.then(V.match_replace(cand2[:, :], best[:, 0:8], cand[:, :], low))
                if part_ == 3:
                    settle(dve)
                    own.then(V.max(best[:, 8:16], cand2[:, :]))
                    settle(dve)
                    own.did(V.max_index(pos[:, 8:16], best[:, 8:16], cand2[:, :]))
                    V.tensor_scalar(nbest[:, :], best[:, 0:1], -1.0, None, ALU.mult).then_inc(best_ready, 1)
                    own.wait()
                    own.did(V.tensor_scalar(pos2[:, 0:TOPK], pos[:, :], 4, None, ALU.logical_shift_right))
                    own.then(V.tensor_scalar(pos2[:, TOPK:2 * TOPK], pos[:, :], TOPK - 1, None, ALU.bitwise_and))
                eq_ = eq[:, :].rearrange("p (c k a) -> p (c k) a", c=2, k=TOPK)
                eq4 = eq[:, :].rearrange("p (c k a) -> p c k a", c=2, k=TOPK)
                if part_ == 4:
                    own.then(V.tensor_tensor(eq_, pos2[:, :].unsqueeze(2).to_broadcast([P, 2 * TOPK, TOPK]),
                                             iota16[:, :].unsqueeze(1).to_broadcast([P, 2 * TOPK, TOPK]), ALU.is_equal))
                    own.then(V.tensor_tensor(eq4, eq4, topf_.unsqueeze(2).to_broadcast([P, 2, TOPK, TOPK]), ALU.mult))
                    own.then(V.tensor_reduce(sel[:, :], eq_, AX.X, ALU.add))
                if part_ in (5, 7):
                    i = (part_ - 5) // 2
                    V.scalar_tensor_tensor(out=idx[i][:, :], in0=sel[:, i * RING:(i + 1) * RING], scalar=float(KEYS),
                                           in1=sel[:, TOPK + i * RING:TOPK + (i + 1) * RING],
                                           op0=ALU.mult, op1=ALU.add).then_inc(routed[i], 1)
                if part_ == 6:
                    dve.wait_ge(exp_ready, H + 1)
                    own.then(V.reciprocal(e_inv[:, :], e_sum[:, :]))
                    held(dve, g_taken, H)
                    V.tensor_scalar(g_next[:, :], e_g[:, :], e_inv[:, :], None, ALU.mult).then_inc(g_ready, 1)

            OWN_PER_ROUTE = 6 + 6 + 4 + 4 + 3 + 1

            def dots(p, H, k):
                b = k % RING
                dve.wait_ge(row_in[b], H * 32 + 16 * (k // RING + 1))
                u = ring[:, b * 2 * D:b * 2 * D + D]
                V.tensor_tensor_reduce(out=u, in0=xn[p % 2], in1=u, scale=1.0, scalar=0.0,
                                       op0=ALU.mult, op1=ALU.add, accum_out=dot[:, k:k + 1]).then_inc(dot_ready, 1)

            def peer_start(p):
                r = rms(xt(p % TILES), D)
                dve.wait_ge(gain_in[p % 2], 16 * (p // 2 + 1))
                V.scalar_tensor_tensor(out=xn[p % 2], in0=xt(p % TILES), scalar=r, in1=xn[p % 2], op0=ALU.mult, op1=ALU.mult)\
                 .then_inc(xn_ready, 1)
                dve.wait_ge(xn_ready, p + 1)

            ROUTE_AT = {4: (0,), 5: (1,), 6: (2,), 7: (3,), 8: (4, 5), 10: (6,)}

            def peer_head(p, H, N, layer, first_of=None, beside=None, s=0):
                for k in range(TOPK):
                    dots(p, H, k)
                    if N is not None:
                        for part_ in ROUTE_AT.get(k, ()):
                            route(N, layer, part_)
                    if first_of is not None and k in TAP_SLOTS:
                        tap(p - 1, 1, first_of + TAP_SLOTS.index(k))
                    if beside is not None:
                        beside(s + k)
                if N is not None:
                    route(N, layer, 7)

            def beside_attention(s):
                if s == 1:
                    latents(1)
                if s == 9:
                    rotate_key(1)
                if s == 11:
                    rotate_moba(1, OFF_MQ)
                if s == 12:
                    rotate_moba(1, OFF_MK)
                if s == 14:
                    rotate_queries(1)
                if s == HEAD_SLOT - 1:
                    maximum(1, 0)
                a, r = divmod(s - HEAD_SLOT, 3)
                if 0 <= a < ATTN_HEADS and r == 1:
                    turn_weights(1, a)
                    if a + 1 < ATTN_HEADS:
                        maximum(1, a + 1)
                if 0 < a <= ATTN_HEADS and r == 0:
                    normalise(1, a - 1)
                if s in (80, 82):
                    mix_out(1, (s - 80) // 2)
                beside_norm(0, s)

            def beside_conv(p, s):
                t = p - 1
                if s == 2:
                    conv_norm_in(t)
                if s - 2 in GLU_SLOTS:
                    glu(t, GLU_SLOTS.index(s - 2))
                for g in range(2):
                    if s == TAPS_AT[g]:
                        first_tap(t, g)
                if 0 < s - TAPS_AT[0] < TAPS:
                    tap(t, 0, s - TAPS_AT[0])
                if s == 89:
                    conv_norm(t)
                if s == 97:
                    conv_out(t, 0)
                if s == 107:
                    conv_out(t, 1)
                beside_norm(p, s)

            def beside_norm(p, s):
                if s == 108:
                    peer_start(p + 1)

            def heads(p, h0, h1, taps=False):
                per = OWN_PER_ROUTE + (KD // 2 * len(TAP_SLOTS) if taps else 0)
                with dve.Fori(h0, h1) as h:
                    with own.loop(h - h0, h1 - h0, per):
                        peer_head(p, h + p * HEADS, h + (p * HEADS + 1), p // TILES, (h - h0) * len(TAP_SLOTS) + 1 if taps else None)

            def busy_heads(p, h0, h1, beside):
                for h in range(h0, h1):
                    peer_head(p, h + p * HEADS, h + p * HEADS + 1, p // TILES, beside=beside, s=h * TOPK)

            def peer_end(p):
                dve.wait_ge(ring_free, RING + (p + 1) * SLOTS)
                V.tensor_copy(xt(p % TILES), ypsum[:, :]).then_inc(y_taken, 1)
                dve.wait_ge(y_taken, p + 1)

            def last_head(p):
                N = (p + 1) * HEADS
                peer_head(p, N - 1, N if p + 1 < PHASES else None, (p + 1) // TILES)
                peer_end(p)

            def final(t):
                r = rms(xt(t), D)
                dve.wait_ge(gain_in[PHASES % 2], 16 * (PHASES // 2 + 1))
                V.scalar_tensor_tensor(out=xt(t), in0=xt(t), scalar=r, in1=xn[PHASES % 2], op0=ALU.mult, op1=ALU.mult)\
                 .then_inc(final_ready, 1)

            project(0)
            project(1)
            dve.wait_ge(consts_in, 6 * 16)
            own.did(V.tensor_copy(mask16[:, :], eq[:, 0:SEQ]))
            V.tensor_copy(ident16[:, :], ident[:, :]).then_inc(id_ready, 1)
            own.then(V.tensor_copy(posf[:, :], posi[:, :]))
            C1 = 6.28125
            C2 = float(np.float32(np.int32(np.float64(2 * np.pi - C1) * 2 ** 20) / 2 ** 20))
            C3 = float(np.float32(2 * np.pi - C1 - C2))
            magic = 12582912.0
            turns, ang = eq[:, 256:256 + 2 * NF], eq[:, 384:384 + 2 * NF]
            for t in range(TILES):
                for c in range(2):
                    own.did(V.tensor_scalar(ang[:, c * NF:(c + 1) * NF], inv[:, :], posf[:, t:t + 1], None, ALU.mult))
                own.wait()
                for c, quarter in ((0, 0.25), (1, 0.0)):
                    s = slice(c * NF, (c + 1) * NF)
                    own.then(V.tensor_scalar(turns[:, s], ang[:, s], float(1 / (2 * np.pi)), quarter, ALU.mult, ALU.add))
                    own.then(V.tensor_scalar(turns[:, s], turns[:, s], magic, -magic, ALU.add, ALU.add))
                    for part_ in (C1, C2, C3):
                        own.then(V.scalar_tensor_tensor(out=ang[:, s], in0=turns[:, s], scalar=-part_, in1=ang[:, s], op0=ALU.mult, op1=ALU.add))
                    if c == 0:
                        own.then(V.tensor_scalar(ang[:, s], ang[:, s], float(np.pi / 2), None, ALU.add))
                own.then(V.tensor_scalar(trig[:, t * 2 * NF:(t + 1) * 2 * NF], ang, 3.1415925, -3.1415925, ALU.min, ALU.max))
            dve.sem_inc(id_ready, 1)
            latents(0)
            rotate_key(0)
            rotate_moba(0, OFF_MQ)
            rotate_moba(0, OFF_MK)
            rotate_queries(0)
            maximum(0, 0)
            for a in range(ATTN_HEADS):
                turn_weights(0, a)
                if a + 1 < ATTN_HEADS:
                    maximum(0, a + 1)
                normalise(0, a)
            dve.wait_ge(out_ready, 1)
            V.tensor_tensor(xt(0), xt(0), ypsum[:, :], ALU.add).then_inc(x_mixed, 1)
            dve.wait_ge(x_mixed, 1)
            peer_start(0)
            for part_ in (0, 1, 2, 3, 4, 5, 7, 6):
                route(0, 0, part_)
            busy_heads(0, 0, 7, beside_attention)
            last_head(0)
            for p in (1, 2):
                busy_heads(p, 0, 3, lambda s: beside_conv(p, s))
                heads(p, 3, 5, taps=True)
                taps_done()
                busy_heads(p, 5, 7, lambda s: beside_conv(p, s))
                last_head(p)
            heads(3, 0, 5)
            final(0)
            heads(3, 5, 7)
            last_head(3)
            final(1)


def kernel(**inputs):
    import concourse.bacc as bacc
    from concourse.bass_utils import run_bass_kernel_spmd

    a = {k: np.asarray(v) for k, v in inputs.items()}

    def rows(w):
        return w.reshape(-1, P, w.shape[1]).transpose(1, 0, 2).reshape(P, -1)

    def split(w):
        return np.ascontiguousarray(w.reshape(-1, P).T)

    taps = a["conv_w_dw"][0].reshape(TAPS, KD, P).transpose(2, 1, 0).reshape(P, KD * TAPS)
    cols = np.concatenate([split(a["norm_mix"]), split(a["conv_b_in"]), split(a["conv_b_dw"]), split(a["conv_ln_g"]),
                           split(a["conv_ln_b"]), split(a["mla_q_norm"]), split(a["mla_kv_norm"]), taps], axis=1)
    f = np.float32
    inv = np.concatenate([f(1.0) / (f(THETA) ** (np.arange(0, d, 2, dtype=f) / f(d))) for d in (ROPE, HD)])
    const = np.concatenate([np.eye(P, dtype=f), np.tile(np.arange(TOPK, dtype=f), (P, 1)), np.tile(inv.astype(f), (P, 1))], axis=1)
    mask = np.concatenate([np.zeros((P, P), f), np.triu(np.full((P, P), -1e30, f), 1)], axis=1)
    ukv = a["mla_w_ukv"][0].reshape(KV_LORA, HEADS, 2, NOPE).transpose(0, 2, 1, 3).reshape(KV_LORA, D)
    wq = a["peer_w_q"].reshape(LAYERS, KD, P, HEADS, 2 * HALF).transpose(0, 3, 2, 1, 4).reshape(LAYERS, HEADS, P, KD * 2 * HALF)
    sk = a["peer_subkeys"].transpose(0, 1, 4, 2, 3).reshape(LAYERS, HEADS, HALF, 2 * KEYS)
    heads = np.concatenate([wq, sk], axis=3)
    arrays = {
        "x": a["x"].reshape(SEQ, D),
        "positions": np.ascontiguousarray(a["positions"].reshape(TILES, P).T),
        "cols": cols, "const": const, "mask": mask,
        "w_in": np.concatenate([rows(a["attn_w_in"][0][:, n:n + w]) for n, w in PROJ_CHUNKS], axis=1),
        "w_uq": rows(a["mla_w_uq"][0]), "w_ukv": rows(ukv), "w_out": rows(a["attn_w_out"][0]),
        "c_in": a["conv_w_in"][0].reshape(KD, P, 2, 4, 256).transpose(1, 3, 0, 2, 4).reshape(P, -1),
        "c_out": np.concatenate([rows(a["conv_w_out"][0][:, n:n + CHUNK]) for n in (0, CHUNK)], axis=1), "c_bout": a["conv_b_out"],
        "heads": heads.transpose(0, 2, 1, 3).reshape(LAYERS, P, HEADS * HEAD_W),
        "gains": np.concatenate([a["norm_ffn"], a["norm_final"].reshape(1, D)], axis=0),
        "table": np.concatenate([a["peer_u"], a["peer_v"]], axis=2).reshape(LAYERS * EXPERTS, 2 * D),
    }
    arrays = {k: np.ascontiguousarray(v) for k, v in arrays.items()}
    nc = bacc.Bacc("TRN2", target_bir_lowering=False, num_devices=1)
    args = [nc.dram_tensor(f"{k}_dram", v.shape, mybir.dt.from_np(v.dtype), kind="ExternalInput").ap() for k, v in arrays.items()]
    out = nc.dram_tensor("out_dram", (SEQ, D), mybir.dt.float32, kind="ExternalOutput").ap()
    build(nc, *args, out)
    r = run_bass_kernel_spmd(nc, [{f"{k}_dram": v for k, v in arrays.items()}], core_ids=[0])
    return r.results[0]["out_dram"].reshape(1, SEQ, D)
```
